# Optimizing a Trainium2 kernel written in Bass

```python
import math
import jax, jax.numpy as jnp
from jax import lax
import numpy as np

D_MODEL = 1024
BATCH = 1
SEQ = 2048
DEPTH = 1
DEC_BATCH = 1
DEC_SEQ = 64
PAST_LEN = 512

CHUNK = 64
N_BAND_PAST = 8
BAND_PAST = N_BAND_PAST * CHUNK
N_HEADS_A = 8
HEAD_DIM = 64
D_ATTN = N_HEADS_A * HEAD_DIM
MAX_REL = 256
N_REL = 2 * MAX_REL + 1
D_RNN = 512
N_RNN_BLOCKS = 8
RNN_BLOCK = D_RNN // N_RNN_BLOCKS
CONV_W = 4
RG_C = 8.0
D_FF = 2816
FFN_CONV_W = 3
EPS = 1e-6
NEG_INF = -1e30
D_IN = 3 * D_ATTN + 2 * D_RNN + 2 * D_MODEL
SPLIT_POINTS = (D_ATTN, 2 * D_ATTN, 3 * D_ATTN, 3 * D_ATTN + D_RNN,
                3 * D_ATTN + 2 * D_RNN, 3 * D_ATTN + 2 * D_RNN + D_MODEL)

kernel_name = "hybrid_chunk_band_rglru_convffn_step"

def rmsnorm(x, g):
    xf = x.astype(jnp.float32)
    y = xf * lax.rsqrt(jnp.mean(xf * xf, axis=-1, keepdims=True) + EPS)
    return (y * g.astype(jnp.float32)).astype(x.dtype)

def adaln(c, w, b):
    m = jax.nn.silu(c) @ w + b
    return jnp.split(m, 3, axis=-1)

def modulate(x, g, shift, scale):
    return rmsnorm(x, g) * (1 + scale[:, None, :]) + shift[:, None, :]

def causal_dwconv(x, prev, w, b):
    width = w.shape[0]
    T = x.shape[1]
    xp = jnp.concatenate([prev, x], axis=1)
    y = b + sum(xp[:, j:j + T] * w[j] for j in range(width))
    return y, xp[:, xp.shape[1] - (width - 1):]

def band_bias(table, n_q, n_past, n_k):
    rel = n_past + jnp.arange(n_q)[:, None] - jnp.arange(n_k)[None, :]
    idx = jnp.clip(rel, -MAX_REL, MAX_REL) + MAX_REL
    return jnp.transpose(table[idx], (2, 0, 1))

def band_attend(q, kb, vb, bias, key_valid):
    s = jnp.einsum('bnthd,bnmhd->bnhtm', q, kb).astype(jnp.float32) * (HEAD_DIM ** -0.5)
    s = s + bias.astype(jnp.float32)[None, None]
    s = jnp.where(key_valid[None, :, None, None, :], s, NEG_INF)
    p = jax.nn.softmax(s, axis=-1).astype(vb.dtype)
    return jnp.einsum('bnhtm,bnmhd->bnthd', p, vb)

def mixer_a_prompt(q, k, v, table):
    B, S, H, dh = q.shape
    nc = S // CHUNK
    nb = N_BAND_PAST + 1
    pad = jnp.zeros((B, BAND_PAST, H, dh), k.dtype)
    kc = jnp.concatenate([pad, k], axis=1).reshape(B, nc + N_BAND_PAST, CHUNK, H, dh)
    vc = jnp.concatenate([pad, v], axis=1).reshape(B, nc + N_BAND_PAST, CHUNK, H, dh)
    idx = jnp.arange(nc)[:, None] + jnp.arange(nb)[None, :]
    kb = kc[:, idx].reshape(B, nc, nb * CHUNK, H, dh)
    vb = vc[:, idx].reshape(B, nc, nb * CHUNK, H, dh)
    valid = jnp.repeat(idx >= N_BAND_PAST, CHUNK, axis=1)
    bias = band_bias(table, CHUNK, BAND_PAST, nb * CHUNK)
    o = band_attend(q.reshape(B, nc, CHUNK, H, dh), kb, vb, bias, valid)
    rows = min(BAND_PAST, S)
    return o.reshape(B, S, H * dh), k[:, S - rows:], v[:, S - rows:]

def mixer_a_sample(q, k, v, past_k, past_v, table):
    B, T, H, dh = q.shape
    P = past_k.shape[1]
    kk = jnp.concatenate([past_k, k], axis=1)[:, None]
    vv = jnp.concatenate([past_v, v], axis=1)[:, None]
    valid = jnp.ones((1, P + T), dtype=bool)
    bias = band_bias(table, T, P, P + T)
    o = band_attend(q[:, None], kk, vv, bias, valid)[:, 0]
    return o.reshape(B, T, H * dh), k, v

def _lin_combine(left, right):
    a1, b1 = left
    a2, b2 = right
    return a1 * a2, a2 * b1 + b2

def rg_lru(x, h0, wa, ba, wx, bx, lam):
    B, T, _ = x.shape
    xb = x.reshape(B, T, N_RNN_BLOCKS, RNN_BLOCK)
    r = jax.nn.sigmoid((jnp.einsum('btni,nij->btnj', xb, wa).reshape(B, T, D_RNN) + ba).astype(jnp.float32))
    ig = jax.nn.sigmoid((jnp.einsum('btni,nij->btnj', xb, wx).reshape(B, T, D_RNN) + bx).astype(jnp.float32))
    log_a = -RG_C * r * jax.nn.softplus(-lam.astype(jnp.float32))
    a = jnp.exp(log_a)
    u = jnp.sqrt(-jnp.expm1(2.0 * log_a)) * (ig * x.astype(jnp.float32))
    u = u.at[:, 0].add(a[:, 0] * h0.astype(jnp.float32))
    _, hs = lax.associative_scan(_lin_combine, (a, u), axis=1)
    return hs.astype(x.dtype), hs[:, -1].astype(x.dtype)

def setup_inputs(seed: int = 0) -> dict:
    key = jax.random.key(seed)
    ks = iter(jax.random.split(key, 40))
    f32 = jnp.float32
    nrm = lambda shape, s: s * jax.random.normal(next(ks), shape, f32)
    a_rows = min(BAND_PAST, PAST_LEN)
    u = jax.random.uniform(next(ks), (DEPTH, D_RNN), f32, 0.9, 0.999)
    a0 = u ** (1.0 / RG_C)
    lam = jnp.log(a0) - jnp.log1p(-a0)
    return {
        "x_prompt": nrm((BATCH, SEQ, D_MODEL), 1.0),
        "x_sample": nrm((DEC_BATCH, DEC_SEQ, D_MODEL), 1.0),
        "c_prompt": nrm((BATCH, D_MODEL), 1.0),
        "c_sample": nrm((DEC_BATCH, D_MODEL), 1.0),
        "cache_k": nrm((DEPTH, DEC_BATCH, a_rows, N_HEADS_A, HEAD_DIM), 1.0),
        "cache_v": nrm((DEPTH, DEC_BATCH, a_rows, N_HEADS_A, HEAD_DIM), 1.0),
        "state_rnn_conv": nrm((DEPTH, DEC_BATCH, CONV_W - 1, D_RNN), 1.0),
        "state_rnn_h": nrm((DEPTH, DEC_BATCH, D_RNN), 0.5),
        "state_ffn_conv": nrm((DEPTH, DEC_BATCH, FFN_CONV_W - 1, 2 * D_FF), 1.0),
        "mod_mix_w": nrm((DEPTH, D_MODEL, 3 * D_MODEL), 0.5 * D_MODEL ** -0.5),
        "mod_mix_b": nrm((DEPTH, 3 * D_MODEL), 0.02),
        "norm_mix_g": 1.0 + nrm((DEPTH, D_MODEL), 0.05),
        "w_in": nrm((DEPTH, D_MODEL, D_IN), D_MODEL ** -0.5),
        "rel_bias_table": nrm((DEPTH, N_REL, N_HEADS_A), 0.2),
        "rnn_conv_w": nrm((DEPTH, CONV_W, D_RNN), CONV_W ** -0.5),
        "rnn_conv_b": nrm((DEPTH, D_RNN), 0.02),
        "rnn_gate_a_w": nrm((DEPTH, N_RNN_BLOCKS, RNN_BLOCK, RNN_BLOCK), RNN_BLOCK ** -0.5),
        "rnn_gate_a_b": nrm((DEPTH, D_RNN), 0.02),
        "rnn_gate_x_w": nrm((DEPTH, N_RNN_BLOCKS, RNN_BLOCK, RNN_BLOCK), RNN_BLOCK ** -0.5),
        "rnn_gate_x_b": nrm((DEPTH, D_RNN), 0.02),
        "rnn_lambda": lam,
        "w_branch": nrm((DEPTH, D_ATTN + D_RNN, D_MODEL), D_RNN ** -0.5),
        "w_out": nrm((DEPTH, D_MODEL, D_MODEL), D_MODEL ** -0.5),
        "mod_ffn_w": nrm((DEPTH, D_MODEL, 3 * D_MODEL), 0.5 * D_MODEL ** -0.5),
        "mod_ffn_b": nrm((DEPTH, 3 * D_MODEL), 0.02),
        "norm_ffn_g": 1.0 + nrm((DEPTH, D_MODEL), 0.05),
        "ffn_up_w": nrm((DEPTH, D_MODEL, 2 * D_FF), D_MODEL ** -0.5),
        "ffn_conv_w": nrm((DEPTH, FFN_CONV_W, 2 * D_FF), FFN_CONV_W ** -0.5),
        "ffn_conv_b": nrm((DEPTH, 2 * D_FF), 0.02),
        "ffn_down_w": nrm((DEPTH, D_FF, D_MODEL), D_FF ** -0.5),
        "final_norm_g": 1.0 + nrm((D_MODEL,), 0.05),
    }

def reference(x_prompt, x_sample, c_prompt, c_sample, cache_k, cache_v, state_rnn_conv,
              state_rnn_h, state_ffn_conv, mod_mix_w, mod_mix_b, norm_mix_g, w_in,
              rel_bias_table, rnn_conv_w, rnn_conv_b, rnn_gate_a_w, rnn_gate_a_b,
              rnn_gate_x_w, rnn_gate_x_b, rnn_lambda, w_branch, w_out, mod_ffn_w, mod_ffn_b,
              norm_ffn_g, ffn_up_w, ffn_conv_w, ffn_conv_b, ffn_down_w, final_norm_g):

    def run(x, c, past_k, past_v, conv_r, h_r, conv_f):
        B, T, _ = x.shape
        ks_, vs_, crs, hs_, cfs = [], [], [], [], []
        for l in range(DEPTH):
            shift, scale, gate = adaln(c, mod_mix_w[l], mod_mix_b[l])
            h = modulate(x, norm_mix_g[l], shift, scale)
            q, k, v, rx, rg, ga, gb = jnp.split(h @ w_in[l], SPLIT_POINTS, axis=-1)
            q = q.reshape(B, T, N_HEADS_A, HEAD_DIM)
            k = k.reshape(B, T, N_HEADS_A, HEAD_DIM)
            v = v.reshape(B, T, N_HEADS_A, HEAD_DIM)
            if past_k is None:
                attn, k_new, v_new = mixer_a_prompt(q, k, v, rel_bias_table[l])
                cr_prev = jnp.zeros((B, CONV_W - 1, D_RNN), x.dtype)
                h_prev = jnp.zeros((B, D_RNN), x.dtype)
                cf_prev = jnp.zeros((B, FFN_CONV_W - 1, 2 * D_FF), x.dtype)
            else:
                attn, k_new, v_new = mixer_a_sample(q, k, v, past_k[l], past_v[l], rel_bias_table[l])
                cr_prev, h_prev, cf_prev = conv_r[l], h_r[l], conv_f[l]
            xc, cr_new = causal_dwconv(rx, cr_prev, rnn_conv_w[l], rnn_conv_b[l])
            hseq, h_new = rg_lru(xc, h_prev, rnn_gate_a_w[l], rnn_gate_a_b[l],
                                 rnn_gate_x_w[l], rnn_gate_x_b[l], rnn_lambda[l])
            rnn = hseq * jax.nn.gelu(rg)
            merged = (jax.nn.sigmoid(ga) * (attn @ w_branch[l, :D_ATTN])
                      + jax.nn.sigmoid(gb) * (rnn @ w_branch[l, D_ATTN:]))
            x = x + gate[:, None, :] * (merged @ w_out[l])
            shift, scale, gate = adaln(c, mod_ffn_w[l], mod_ffn_b[l])
            h = modulate(x, norm_ffn_g[l], shift, scale)
            up, cf_new = causal_dwconv(h @ ffn_up_w[l], cf_prev, ffn_conv_w[l], ffn_conv_b[l])
            val, gt = jnp.split(up, 2, axis=-1)
            x = x + gate[:, None, :] * ((val * jax.nn.gelu(gt)) @ ffn_down_w[l])
            ks_.append(k_new); vs_.append(v_new); crs.append(cr_new); hs_.append(h_new); cfs.append(cf_new)
        y = rmsnorm(x, final_norm_g)
        return y, jnp.stack(ks_), jnp.stack(vs_), jnp.stack(crs), jnp.stack(hs_), jnp.stack(cfs)

    y_prompt, k_p, v_p, rc_p, h_p, fc_p = run(x_prompt, c_prompt, None, None, None, None, None)
    y_sample, k_s, v_s, rc_s, h_s, fc_s = run(x_sample, c_sample, cache_k, cache_v,
                                              state_rnn_conv, state_rnn_h, state_ffn_conv)
    return (y_prompt, y_sample, k_p, v_p, k_s, v_s, rc_p, rc_s, h_p, h_s, fc_p, fc_s)


_drawn_inputs = setup_inputs


def setup_inputs(seed=0):
    import zlib

    import numpy as np

    out = dict(_drawn_inputs(seed))
    spreads = {}
    factors = {'cache_k': 6.174,
     'cache_v': 5.041,
     'rel_bias_table': 8.0,
     'rnn_gate_a_b': 8.0,
     'rnn_gate_x_b': 6.527,
     'ffn_conv_b': 8.0}
    for name, (base, spread) in spreads.items():
        noise = np.random.default_rng([zlib.crc32(name.encode()), seed]).standard_normal(out[name].shape)
        drawn = base * np.exp(spread * noise) if base else spread * noise
        out[name] = __import__('jax').numpy.asarray(drawn.astype(out[name].dtype))
    for name, factor in factors.items():
        out[name] = (out[name] * factor).astype(out[name].dtype)
    return out
```

```python
from contextlib import ExitStack

import concourse.bass as bass
from concourse import mybir

ALU = mybir.AluOpType
ACT = mybir.ActivationFunctionType
F32 = mybir.dt.float32
F16 = mybir.dt.float16
ds = bass.ds

P = 128
D = 1024
KT = D // P
TP, TS = 2048, 64
T = TP + TS
NT = TP // P
HD = 64
NJ = 4
PAST = 512
KEYS = TP + PAST + TS
BAND = 640
DFF = 2816
NF = DFF // P
EPS = 1e-6
WS, XS = 256.0, 8.0
CS = 1.0 / (WS * XS)
NEG = -1e30
ARENA = 53200
BLOCKS = [(0, 512), (512, 512), (1024, 512), (1536, 512), (2048, 64)]
PASSES = [(0, 0), (0, 1), (1, 0)]

COLS = {}
NPAR = 0
for _name, _n in (("c", 16), ("mod_b", 48), ("g_mix", 8), ("g_ffn", 8), ("cw", 16), ("cb", 4), ("ba", 4),
                  ("bx", 4), ("lam", 4), ("h0", 4), ("cstate", 12), ("fw", 132), ("fb", 44), ("fstate", 88)):
    COLS[_name] = NPAR
    NPAR += _n

WQ, WK, WV, WRX, WRG, WGA, WGB = 0, 4, 8, 12, 16, 20, 28


def build(nc, a):
    ctx = ExitStack()
    with ctx:
        def sem(name):
            return ctx.enter_context(nc.semaphore(name))

        arena = ctx.enter_context(nc.sbuf_tensor("arena", [P, ARENA], F32))
        ps = ctx.enter_context(nc.psum_tensor("ps", [P, 8, 512], F32))

        def carve(at, n, dt=F32):
            w = n if dt == F32 else (n + 1) // 2
            assert at + w <= ARENA, (at, w)
            v = arena[:, at:at + w]
            return (v if dt == F32 else v.bitcast(dt)), at + w

        at = 0
        hT_, at = carve(at, KT * 2 * T, F16)
        hT = hT_.rearrange("p (k s t) -> p k s t", k=KT, s=2)
        par, at = carve(at, NPAR)
        ident, at = carve(at, P)
        mod, at = carve(at, 96)
        modv = mod.rearrange("p (m f s) -> p m f s", m=2, s=2)
        coef, at = carve(at, 2 * 2 * 2 * KT)
        coefv = coef.rearrange("p (m c s k) -> p m c s k", m=2, c=2, s=2)
        sp8, at = carve(at, 4)
        small, at = carve(at, 64)
        rstd, at = carve(at, 24)
        hold_conv, at = carve(at, 4 * 8)
        holdv = hold_conv.rearrange("p (j c) -> p j c", j=4)
        fhold, at = carve(at, 44 * 4)
        fholdv = fhold.rearrange("p (f c) -> p f c", c=4)
        BASE = at

        def col(name, i=0, n=1):
            c = COLS[name] + i
            return par[:, c:c + n]

        x_all, at = carve(BASE, (NT + 1) * D)
        x_all = x_all.rearrange("p (i d) -> p i d", d=D)
        mw_, at = carve(at, 4 * D)
        mw = mw_.rearrange("p (s k m) -> p s k m", s=4, k=KT)
        xn_, at = carve(at, 2 * D)
        xn = xn_.rearrange("p (s d) -> p s d", s=2)
        tmp_, at = carve(at, 2 * D)
        tmp = tmp_.rearrange("p (s k t) -> p s k t", s=2, k=KT)
        junk_, at = carve(at, 2 * D)
        junk = junk_.rearrange("p (s d) -> p s d", s=2)
        cs, at = carve(at, 16)
        csv = cs.rearrange("p (k s) -> p k s", s=2)
        sgc, at = carve(at, 16)
        gcols, at = carve(at, 32)
        grow, at = carve(at, P)
        tab, at = carve(at, 513)
        tabr, at = carve(at, 768)

        at = BASE
        wst_, at = carve(at, 2 * D)
        wst = wst_.rearrange("p (s k m) -> p s k m", s=2, k=KT)
        wsp_, at = carve(at, 2 * 2 * D, F16)
        wsp = wsp_.rearrange("p (s h k m) -> p s h k m", s=2, h=2, k=KT)
        LB = T + 3
        bufA, at = carve(at, TP + 3 + TS + 3)
        bufX, at = carve(at, LB)
        bufI, at = carve(at, LB)
        bufT, at = carve(at, LB)
        bufG, at = carve(at, LB)
        rstage_, at = carve(at, 2 * LB, F16)
        rstage = rstage_.rearrange("p (s t) -> p s t", s=2)
        bufR, _ = carve(at - LB, LB)
        bias_, at = carve(at, 2 * BAND)
        bias = bias_.rearrange("p (h n) -> p h n", h=2)
        qs_, at = carve(at, 2 * T, F16)
        qs = qs_.rearrange("p (h t) -> p h t", h=2)
        khh_, at = carve(at, 2 * KEYS, F16)
        khh = khh_.rearrange("p (h t) -> p h t", h=2)
        kll_, at = carve(at, 2 * KEYS, F16)
        kll = kll_.rearrange("p (h t) -> p h t", h=2)
        vv_, at = carve(at, 21 * P)
        vv = vv_.rearrange("p (i d) -> p i d", d=P)
        kf, at = carve(at, PAST + TS)
        pr_, at = carve(at, 2 * BAND)
        pr = pr_.rearrange("p (h n) -> p h n", h=2)
        pt_, at = carve(at, 2 * BAND)
        pt = pt_.rearrange("p (h n) -> p h n", h=2)
        osb, at = carve(at, P)
        ost_, at = carve(at, 2 * T, F16)
        ost = ost_.rearrange("p (s t) -> p s t", s=2)
        kc_, at = carve(at, 4 * P)
        kc = kc_.rearrange("p (c d) -> p c d", c=4)
        gw_, at = carve(at, 2 * P)
        gw = gw_.rearrange("p (g m) -> p g m", g=2)
        gbias, at = carve(at, 2)
        mark, at = carve(at, 1)
        mx, at = carve(at, 2)
        nmx, at = carve(at, 2)
        sm, at = carve(at, 2)
        rs, at = carve(at, 2)

        mixT_, at = carve(BASE, KT * 2 * T, F16)
        mixT = mixT_.rearrange("p (k s t) -> p k s t", k=KT, s=2)
        dst_, at = carve(at, 3 * D)
        dst = dst_.rearrange("p (s k m) -> p s k m", s=3, k=KT)
        dsp_, at = carve(at, 6 * 2 * D, F16)
        dsp = dsp_.rearrange("p (s h k m) -> p s h k m", s=6, h=2, k=KT)
        mstage_, at = carve(at, 2 * T, F16)
        mstage = mstage_.rearrange("p (s t) -> p s t", s=2)
        sig_, at = carve(at, 4 * 512)
        sig = sig_.rearrange("p (b g t) -> p b g t", b=2, g=2)
        prod_, at = carve(at, 2 * 512)
        prod = prod_.rearrange("p (g t) -> p g t", g=2)
        mrg_, at = carve(at, 2 * 512)
        mrg = mrg_.rearrange("p (b t) -> p b t", b=2)

        mT_, at = carve(BASE, KT * 2 * T, F16)
        mT = mT_.rearrange("p (k s t) -> p k s t", k=KT, s=2)
        wo_, at = carve(at, KT * 2 * D, F16)
        wo = wo_.rearrange("p (k h m) -> p k h m", k=KT, h=2)
        gate1_, at = carve(at, 2 * D)
        gate1 = gate1_.rearrange("p (s d) -> p s d", s=2)
        ex_, at = carve(at, 2 * D)
        ex = ex_.rearrange("p (b d) -> p b d", b=2)
        exn_, at = carve(at, 2 * D)
        exn = exn_.rearrange("p (b d) -> p b d", b=2)
        est = exn
        etmp_, at = carve(at, 2 * D)
        etmp = etmp_.rearrange("p (s k t) -> p s k t", s=2, k=KT)

        LF = T + 2
        fsp_, at = carve(BASE, 2 * 2 * D, F16)
        fsp = fsp_.rearrange("p (s h k m) -> p s h k m", s=2, h=2, k=KT)
        ubuf, at = carve(at, LF + 2)
        yval, at = carve(at, LF)
        ygate, at = carve(at, LF)
        hstage_, at = carve(at, 2 * LF, F16)
        hstage = hstage_.rearrange("p (s t) -> p s t", s=2)
        fst_, at = carve(at, 2 * D)
        fst = fst_.rearrange("p (s m) -> p s m", s=2)
        wd_, at = carve(at, NF * 2 * D, F16)
        wd = wd_.rearrange("p (k h m) -> p k h m", k=NF, h=2)

        hb0_, at = carve(0, NF * 2 * 512, F16)
        gate2_, at = carve(at, 2 * D)
        gate2 = gate2_.rearrange("p (s d) -> p s d", s=2)
        gfin, at = carve(at, D)
        gx_, at = carve(at, 2 * D)
        gx = gx_.rearrange("p (b d) -> p b d", b=2)
        assert at <= KT * T
        hb1_, at = carve(BASE, NF * 2 * 512, F16)
        assert at <= BASE + 4 * D + LF + 2 + 3 * LF
        hb = [h.rearrange("p (k s t) -> p k s t", k=NF, s=2) for h in (hb0_, hb1_)]

        bias_d = nc.dram_tensor("bias_rows", (8, 768), F32, kind="Internal").ap()
        band_d = nc.dram_tensor("band", (P, 8, BAND), F32, kind="Internal").ap()
        gate_d = nc.dram_tensor("gate_rows", (4, D), F32, kind="Internal").ap()
        mix_d = nc.dram_tensor("mixer_outputs", (8, P, 2, T), F16, kind="Internal").ap()
        merged_d = nc.dram_tensor("merged", (KT, P, 2, T), F16, kind="Internal").ap()
        x1_d = nc.dram_tensor("x_after_mixers", (T, D), F32, kind="Internal").ap()
        hid_d = nc.dram_tensor("ffn_hidden", (NF, P, 2, T), F16, kind="Internal").ap()

        par_loaded = sem("par_loaded")
        tab_loaded = sem("tab_loaded")
        tab_ready = sem("tab_ready")
        bias_rows_stored = sem("bias_rows_stored")
        band_stored = sem("band_stored")
        x_loaded = [sem(f"x_loaded{i}") for i in range(5)]
        mw_loaded = [sem(f"mw_loaded{i}") for i in range(4)]
        ident_ready = sem("ident_ready")
        silu_sig = sem("silu_sig")
        silu_ready = sem("silu_ready")
        mod_filled = sem("mod_filled")
        dve_seq = sem("dve_seq")
        coef_ready = sem("coef_ready")
        ss_ready = sem("ss_ready")
        var_ready = sem("var_ready")
        std_ready = sem("std_ready")
        rstd_ready = sem("rstd_ready")
        xn_ready = sem("xn_ready")
        xT_filled = sem("xT_filled")
        tmp_ready = sem("tmp_ready")
        hi_ready = sem("hi_ready")
        hT_ready = sem("hT_ready")
        gcols_ready = sem("gcols_ready")
        grow_filled = sem("grow_filled")
        grow_ready = sem("grow_ready")
        gate_rows_stored = sem("gate_rows_stored")
        sp_a = sem("sp_a")
        sp_v = sem("sp_v")

        st_loaded = [sem(f"st_loaded{i}") for i in range(2)]
        w_hi = sem("w_hi")
        w_split = sem("w_split")
        gw_zero = sem("gw_zero")
        gw_loaded = sem("gw_loaded")
        aux_loaded = sem("aux_loaded")
        kc_loaded = sem("kc_loaded")
        v_loaded = sem("v_loaded")
        gap_ready = sem("gap_ready")
        c_filled = sem("c_filled")
        c_act = sem("c_act")
        c_dve = sem("c_dve")
        c_hi = sem("c_hi")
        kdup = sem("kdup")
        xc_ready = sem("xc_ready")
        rg_act = sem("rg_act")
        rg_dve = sem("rg_dve")
        kf_ready = sem("kf_ready")
        kf_stored = sem("kf_stored")
        v_stored = sem("v_stored")
        rnn_stored = sem("rnn_stored")
        attn_stored = sem("attn_stored")
        held = sem("held")
        hold_stored = sem("hold_stored")
        s_filled = sem("s_filled")
        s_added = sem("s_added")
        s_negmax = sem("s_negmax")
        p_ready = sem("p_ready")
        r_ready = sem("r_ready")
        t_filled = sem("t_filled")
        t_act = sem("t_act")
        t_dve = sem("t_dve")
        o_filled = sem("o_filled")
        o_ready = sem("o_ready")
        ot_filled = sem("ot_filled")
        ot_hi = sem("ot_hi")
        ot_ready = sem("ot_ready")
        bias_masked = sem("bias_masked")

        d_loaded = [sem(f"d_loaded{i}") for i in range(3)]
        mix_loaded = sem("mix_loaded")
        d_hi = sem("d_hi")
        d_split = sem("d_split")
        d_filled = sem("d_filled")
        d_act = sem("d_act")
        d_dve = sem("d_dve")
        d_step = sem("d_step")
        d_mhi = sem("d_mhi")
        d_mlo = sem("d_mlo")
        m_stored = sem("m_stored")

        e_loaded = [sem(f"e_loaded{i}") for i in range(2)]
        e_whi = sem("e_whi")
        e_split = sem("e_split")
        m_loaded = [sem(f"m_loaded{i}") for i in range(5)]
        gate1_loaded = sem("gate1_loaded")
        ex_loaded = [sem(f"ex_loaded{i}") for i in range(2)]
        x1_stored = [sem(f"x1_stored{i}") for i in range(2)]
        e_filled = sem("e_filled")
        e_gated = sem("e_gated")
        e_evac = sem("e_evac")
        e_ss = sem("e_ss")
        e_var = sem("e_var")
        e_std = sem("e_std")
        e_rstd = sem("e_rstd")
        e_xn = sem("e_xn")
        e_xt = sem("e_xt")
        e_tmp = sem("e_tmp")
        e_hi = sem("e_hi")
        e_hT = sem("e_hT")

        f_loaded = [sem(f"f_loaded{i}") for i in range(2)]
        f_hi = sem("f_hi")
        f_split = sem("f_split")
        f_filled = sem("f_filled")
        f_pad = sem("f_pad")
        f_act = sem("f_act")
        f_conv = sem("f_conv")
        f_gelu = sem("f_gelu")
        f_prod = sem("f_prod")
        f_phi = sem("f_phi")
        f_plo = sem("f_plo")
        h_stored = sem("h_stored")

        hb_loaded = [[sem(f"hb_loaded{s}{q}") for q in range(2)] for s in range(2)]
        hs_loaded = sem("hs_loaded")
        rows_loaded = sem("rows_loaded")
        gx_loaded = [sem(f"gx_loaded{i}") for i in range(2)]
        g_filled = sem("g_filled")
        g_gated = sem("g_gated")
        g_evac = sem("g_evac")
        g_ss = sem("g_ss")
        g_var = sem("g_var")
        g_std = sem("g_std")
        g_rstd = sem("g_rstd")
        g_y = sem("g_y")
        y_stored = [sem(f"y_stored{i}") for i in range(2)]

        block = ctx.enter_context(nc.Block())

        UNITS = [(WRX, 0), (WRG, 1), (WQ, 0), (WK, 1), (WV, 0)]
        USES = (["A"] * 5 + ["A"] * 5 + ["V"] * 5 + ["A"] * 10 + ["V"] * 5 + ["V"] + ["V"] * 5)
        NU = len(USES)
        NA, NV = USES.count("A"), USES.count("V")
        U_RX, U_RG, U_Q, U_G, U_K, U_KC, U_V = 0, 5, 10, 15, 25, 30, 31

        def drained_before(u):
            e = USES[u]
            return e, USES[:u + 1].count(e)

        def short(p):
            n = P * (p + 1)
            return 0, n, BAND - n

        NUNIT = 2 * (NT + 1)

        @block.sync
        def _(sp):
            sp.dma_start(par, a["params"]).then_inc(par_loaded, 16)
            sp.dma_start(tab[0:8, :], a["rel_table"]).then_inc(tab_loaded, 16)
            xp = a["x_prompt"].rearrange("(g i p) d -> g p i d", p=P, i=4)
            for g in range(4):
                sp.dma_start(x_all[:, 4 * g:4 * g + 4, :], xp[g]).then_inc(x_loaded[g], 16)
            sp.dma_start(x_all[0:TS, NT, :], a["x_sample"]).then_inc(x_loaded[4], 16)
            with nc.sync.Fori(0, 12) as it:
                for s in range(4):
                    sp.wait_ge(mod_filled, 4 * it + s + 1)
                    sp.dma_start(mw[:, s], a["w_mod"][ds(4 * it + s, 1)].rearrange("a p k m -> p (a k) m"))\
                        .then_inc(mw_loaded[s], 16)

            sp.wait_ge(gate_rows_stored, 16)
            sp.wait_ge(hT_ready, 2 * (NT + 1))
            sp.wait_ge(gw_zero, 1)
            sp.wait_ge(band_stored, 16)
            with nc.sync.Fori(0, NJ) as j:
                for i, (w, s) in enumerate(UNITS):
                    sp.wait_ge(w_split, 5 * j + (5, 4, 6, 7, 8)[i])
                    sp.dma_start(wst[:, s], a["w_in"][ds(j + w, 1)].rearrange("a p k m -> p (a k) m"))\
                        .then_inc(st_loaded[s], 16)
                    if i == 1:
                        sp.wait_ge(c_filled, NU * j + NU)
                        for b in range(2):
                            sp.dma_start(gw[64 * b:64 * b + 64, :, 64 * b:64 * b + 64],
                                         a["w_rgate"][:, ds(2 * j + b, 1)].rearrange("g n i m -> i (g n) m"))\
                                .then_inc(gw_loaded, 16)
                    if i == 2:
                        sp.wait_ge(ot_ready, (NT + 1) * (j + 1))
                        sp.wait_ge(v_stored, 32 * j + 32)
                        sp.dma_start(kc, a["cache_k"][:, :, ds(j, 1), :].rearrange("c p j d -> p (c j) d"))\
                            .then_inc(kc_loaded, 16)
                        sp.dma_start(vv[:, NT:NT + 4, :],
                                     a["cache_v"][:, :, ds(j, 1), :].rearrange("c p j d -> p (c j) d"))\
                            .then_inc(v_loaded, 16)
                        sp.dma_start(bias, band_d[:, ds(2 * j, 2), :]).then_inc(aux_loaded, 16)

            sp.wait_ge(ot_ready, (NT + 1) * (NJ + 1))
            sp.wait_ge(kf_stored, 32 * (NJ + 1))
            sp.wait_ge(v_stored, 32 * (NJ + 1))
            sp.wait_ge(rnn_stored, 32 * (NJ + 1))

            def merge_tiles(it, q):
                for i, src in enumerate((a["w_in"][ds(2 * it + q + WGA, 1)], a["w_in"][ds(2 * it + q + WGB, 1)],
                                         a["w_branch"][ds(2 * it + q, 1)])):
                    sp.wait_ge(d_split, 6 * it + 3 * q + i + 1)
                    sp.dma_start(dst[:, i], src.rearrange("a p k m -> p (a k) m")).then_inc(d_loaded[i], 16)

            merge_tiles(0, 0)
            sp.wait_ge(attn_stored, 16 * (NJ + 1))
            for k in range(KT):
                sp.dma_start(mixT[:, k], mix_d[k]).then_inc(mix_loaded, 16)
            merge_tiles(0, 1)
            with nc.sync.Fori(1, KT // 2) as it:
                for q in range(2):
                    merge_tiles(it, q)

            sp.wait_ge(d_filled, 40 + 20 * KT)
            sp.wait_ge(m_stored, 16 * (KT + 1))
            for n, (t, w) in enumerate(BLOCKS):
                for part in range(2):
                    sp.dma_start(mT[:, :, part, t:t + w], merged_d[:, :, part, t:t + w].rearrange("k p t -> p k t"))\
                        .then_inc(m_loaded[n], 16)
                if n == 0:
                    with nc.sync.Fori(0, KT // 2) as it:
                        for s in range(2):
                            sp.wait_ge(e_split, 2 * it + s + 1)
                            sp.dma_start(est[:, s], a["w_out"][ds(2 * it + s, 1)].rearrange("k p m -> p (k m)"))\
                                .then_inc(e_loaded[s], 16)
                    for s in range(2):
                        sp.dma_start(gate1[:, s, :], gate_d[s:s + 1, :].to_broadcast([P, D])).then_inc(gate1_loaded, 16)
                    for b in range(2):
                        sp.dma_start(ex[:, b], a["x_prompt"][b * P:(b + 1) * P, :]).then_inc(ex_loaded[b], 16)
            with nc.sync.Fori(1, NT // 2) as it:
                for b in range(2):
                    sp.wait_ge(x1_stored[b], 16 * it + 16)
                    sp.wait_ge(e_xn, 2 * it + b - 1)
                    sp.dma_start(ex[:, b], a["x_prompt"][ds(2 * P * it + b * P, P), :]).then_inc(ex_loaded[b], 16)
            sp.wait_ge(x1_stored[0], 16 * (NT // 2) + 16)
            sp.wait_ge(e_xn, NT - 1)
            sp.dma_start(ex[0:TS, 0], a["x_sample"]).then_inc(ex_loaded[0], 16)

            def ffn_tile(src, s):
                sp.dma_start(fst[:, s], src).then_inc(f_loaded[s], 16)

            sp.wait_ge(e_filled, NT + 1)
            ffn_tile(a["w_up"][0].rearrange("p k m -> p (k m)"), 0)

            def ffn_tiles(f, last):
                sp.wait_ge(f_split, 3 * f + 2)
                ffn_tile(a["w_up"][ds(f + NF, 1)].rearrange("a p k m -> p (a k m)"), 1)
                sp.wait_ge(f_split, 3 * f + 4)
                ffn_tile(a["w_down"][ds(f, 1)].rearrange("a p m -> p (a m)"), 0)
                if not last:
                    sp.wait_ge(f_split, 3 * f + 6)
                    ffn_tile(a["w_up"][ds(f + 1, 1)].rearrange("a p k m -> p (a k m)"), 0)

            with nc.sync.Fori(0, NF - 1) as f:
                ffn_tiles(f, False)
            ffn_tiles(NF - 1, True)

            sp.wait_ge(f_filled, 10 * NF + 10)
            sp.wait_ge(h_stored, 32 * NF + 32)
            sp.wait_ge(f_split, 3 * NF + 3)
            sp.wait_ge(x1_stored[0], 16 * (NT // 2 + 2))
            sp.wait_ge(x1_stored[1], 16 * (NT // 2 + 1))

            def hidden(ib, s):
                for q in range(2):
                    for part in range(2):
                        sp.dma_start(hb[s][:, :, part, 256 * q:256 * q + 256],
                                     hid_d[:, :, part, 1024 * ib + 512 * s + 256 * q:
                                           1024 * ib + 512 * s + 256 * q + 256].rearrange("k p t -> p k t"))\
                            .then_inc(hb_loaded[s][q], 16)

            def residual(row, b, rows=P):
                sp.dma_start(gx[0:rows, b], x1_d[ds(row, rows), :]).then_inc(gx_loaded[b], 16)

            hidden(0, 0)
            for s in range(2):
                sp.dma_start(gate2[:, s, :], gate_d[2 + s:3 + s, :].to_broadcast([P, D])).then_inc(rows_loaded, 16)
            sp.dma_start(gfin, a["g_final"].to_broadcast([P, D])).then_inc(rows_loaded, 16)
            residual(0, 0)
            residual(P, 1)
            hidden(0, 1)

            def residuals(i, n):
                for b in range(2):
                    sp.wait_ge(y_stored[b], n)
                    residual(i * P + b * P, b)

            residuals(2, 32)
            residuals(4, 48)
            sp.wait_ge(g_filled, 4)
            hidden(1, 0)
            residuals(6, 64)
            residuals(8, 80)
            sp.wait_ge(g_filled, 8)
            hidden(1, 1)
            residuals(10, 96)
            residuals(12, 112)
            sp.wait_ge(g_filled, 12)
            for part in range(2):
                sp.dma_start(hb[0][:, :, part, 0:TS], hid_d[:, :, part, TP:T].rearrange("k p t -> p k t"))\
                    .then_inc(hs_loaded, 16)
            residuals(14, 128)
            sp.wait_ge(y_stored[0], 16 * (NT // 2 + 1))
            residual(TP, 0, TS)

        @block.gpsimd
        def _(pool):
            pool.memset(ident, 0.0).then_inc(ident_ready, 1)
            pool.wait_ge(ident_ready, 1)
            pool.affine_select(out=ident, in_=ident, compare_op=ALU.not_equal, fill=1.0, base=0,
                               pattern=[[-1, P]], channel_multiplier=1).then_inc(ident_ready, 1)
            pool.wait_ge(tab_ready, 2)
            pool.dma_start(bias_d[:, 0:767], tabr[0:8, 0:767]).then_inc(bias_rows_stored, 16)
            pool.wait_ge(bias_rows_stored, 16)
            pool.dma_start(band_d.rearrange("q h n -> h q n"),
                           bass.AP(bias_d.tensor, P - 1, [[768, 8], [-1, P], [1, BAND]]))\
                .then_inc(band_stored, 16)
            pool.wait_ge(grow_ready, 1)
            pool.dma_start(gate_d.rearrange("g (k p) -> (g k) p", p=P), grow[0:32, :]).then_inc(gate_rows_stored, 16)
            pool.wait_ge(gate_rows_stored, 16)
            pool.wait_ge(hT_ready, 2 * (NT + 1))
            pool.memset(gw, 0.0).then_inc(gw_zero, 1)
            pool.memset(bufI[:, TP:TP + 3], 0.0).then_inc(gap_ready, 1)
            pool.memset(bufG[:, TP:TP + 3], 0.0).then_inc(gap_ready, 1)

        @block.scalar
        def _(act):
            act.wait_ge(par_loaded, 16)
            act.activation(sgc, col("c", 0, 16), ACT.Sigmoid).then_inc(silu_sig, 1)
            act.activation(small[:, 0:4], col("lam", 0, 4), ACT.Abs).then_inc(sp_a, 1)
            act.wait_ge(sp_a, 1)
            act.activation(small[:, 4:8], small[:, 0:4], ACT.Exp, scale=-1.0).then_inc(sp_a, 1)
            for g in range(4):
                act.wait_ge(x_loaded[g], 16)
                for i in range(4 * g, 4 * g + 4):
                    if i >= 2:
                        act.wait_ge(ss_ready, i - 1)
                    act.activation(junk[:, i % 2], x_all[:, i, :], ACT.Square, accum_out=rstd[:, i:i + 1])\
                        .then_inc(ss_ready, 1)
            act.wait_ge(x_loaded[4], 16)
            act.wait_ge(ss_ready, NT - 1)
            act.activation(junk[0:TS, NT % 2], x_all[0:TS, NT, :], ACT.Square, accum_out=rstd[0:TS, NT:NT + 1])\
                .then_inc(ss_ready, 1)
            act.wait_ge(var_ready, 1)
            act.activation(rstd[:, 0:NT + 1], rstd[:, 0:NT + 1], ACT.Sqrt).then_inc(std_ready, 1)

            def norm_tile(i, n, rows, half):
                if n is not None:
                    act.wait_ge(xT_filled, n)
                act.mul(xn[0:rows, half, :], x_all[0:rows, ds(i, 1), :].rearrange("p i d -> p (i d)"),
                        rstd[0:rows, ds(i, 1)]).then_inc(xn_ready, 1)

            def high_tile(i, rows, half):
                for q in range(2):
                    act.wait_ge(tmp_ready, 2 * i + q + 4)
                    act.activation(hT[:, 4 * q:4 * q + 4, 0, ds(i * P, rows)],
                                   tmp[:, half, 4 * q:4 * q + 4, 0:rows], ACT.Copy).then_inc(hi_ready, 1)

            act.wait_ge(rstd_ready, 1)
            with nc.scalar.Fori(0, NT // 2) as it:
                for b in range(2):
                    norm_tile(2 * it + b, 2 * it + b + 1, P, b)
                    high_tile(2 * it + b, P, b)
            norm_tile(NT, NT + 1, TS, 0)
            high_tile(NT, TS, 0)
            act.wait_ge(grow_filled, 1)
            act.copy(grow[0:32, :], ps[0:32, 5, 0:P]).then_inc(grow_ready, 1)

            act.sem_inc(c_act, NA)
            act.sem_inc(kf_stored, 32)
            act.sem_inc(v_stored, 32)
            act.sem_inc(rnn_stored, 32)
            act.sem_inc(attn_stored, 16)
            act.wait_ge(gate_rows_stored, 16)
            act.wait_ge(gap_ready, 2)
            act.wait_ge(hT_ready, 2 * (NT + 1))
            with nc.scalar.Fori(0, NJ) as j:
                def split_hi(i):
                    s = UNITS[i][1]
                    v = (3 * j + i // 2 + 1) if s == 0 else (2 * j + i // 2 + 1)
                    act.wait_ge(st_loaded[s], 16 * v)
                    if i >= 2:
                        act.wait_ge(c_filled, NU * j + NU + (5, 10, 15)[i - 2])
                    act.activation(wsp[:, s, 0], wst[:, s], ACT.Copy, scale=WS).then_inc(w_hi, 1)

                def filled(u):
                    act.wait_ge(c_filled, NU * j + NU + u + 1)
                    return ps[:, u % 8, :]

                split_hi(0)
                split_hi(1)
                act.activation(bufA[:, 0:3], ident[:, 0:3], ACT.Copy, scale=0.0).then_inc(rg_act, 1)
                act.activation(bufA[:, TP + 3:TP + 6].rearrange("p (a b) -> p a b", a=1),
                               col("cstate", 0, 12).rearrange("p (j b) -> p j b", b=3)[:, ds(j, 1), :],
                               ACT.Copy).then_inc(rg_act, 1)
                for n, (t, w) in enumerate(BLOCKS):
                    o = 3 if t < TP else 6
                    act.activation(bufA[:, t + o:t + o + w], filled(U_RX + n)[:, 0:w], ACT.Copy, scale=CS)\
                        .then_inc(c_act, 1)
                split_hi(2)
                for n, (t, w) in enumerate(BLOCKS):
                    o = 0 if t < TP else 3
                    act.activation(bufG[:, t + o:t + o + w], filled(U_RG + n)[:, 0:w], ACT.Gelu_apprx_tanh,
                                   scale=CS).then_inc(c_act, 1)
                split_hi(3)
                for n, (t, w) in enumerate(BLOCKS):
                    src = filled(U_Q + n)
                    act.activation(qs[0:64, 0, t:t + w], src[0:64, 0:w], ACT.Copy, scale=CS * HD ** -0.5)
                    act.activation(qs[64:128, 1, t:t + w], src[64:128, 0:w], ACT.Copy, scale=CS * HD ** -0.5)\
                        .then_inc(c_hi, 1)
                split_hi(4)
                for n, (t, w) in enumerate(BLOCKS):
                    o = 0 if t < TP else 3
                    for g, gate in enumerate((bufA, bufI)):
                        act.activation(gate[:, t + o:t + o + w], filled(U_G + 2 * n + g)[:, 0:w], ACT.Sigmoid,
                                       bias=gbias[:, g:g + 1]).then_inc(c_act, 1)

                def k_hi(n):
                    if n < 5:
                        t, w = BLOCKS[n]
                        kt, u, sc = (t if t < TP else TP + PAST), U_K + n, CS
                    else:
                        kt, w, u, sc = TP, PAST, U_KC, 1.0
                    src = filled(u)
                    if n == 3:
                        act.wait_ge(kf_stored, 32 * j + 32)
                    if n == 3 or n == 4:
                        o = 0 if n == 3 else PAST
                        act.activation(kf[:, o:o + w], src[:, 0:w], ACT.Copy, scale=CS).then_inc(kf_ready, 1)
                    for h in range(2):
                        own = slice(64 * h, 64 * h + 64)
                        k = act.activation(khh[own, h, kt:kt + w], src[own, 0:w], ACT.Copy, scale=sc)
                    k.then_inc(c_hi, 1)

                k_hi(0)
                k_hi(1)
                act.wait_ge(rg_dve, 10 * j + 2)
                act.activation(bufT[:, 0:LB], bufA[:, 0:LB], ACT.Tanh).then_inc(rg_act, 1)
                act.activation(bufA[:, 0:LB], bufA[:, 0:LB], ACT.Exp, scale=-1.0).then_inc(rg_act, 1)
                k_hi(2)
                k_hi(3)
                act.wait_ge(rg_dve, 10 * j + 5)
                act.activation(bufT[:, 0:LB], bufT[:, 0:LB], ACT.Sqrt).then_inc(rg_act, 1)
                k_hi(4)
                k_hi(5)
                act.wait_ge(rg_dve, 10 * j + 9)
                act.wait_ge(rnn_stored, 32 * j + 32)
                act.activation(rstage[:, 0, :], bufX, ACT.Copy, scale=XS).then_inc(rg_act, 1)

                act.dma_start(a["k_prompt"][ds(j, 1)].rearrange("j p t -> (j p) t"), kf[:, 0:PAST])\
                    .then_inc(kf_stored, 16)
                act.dma_start(a["k_sample"][ds(j, 1)].rearrange("j p t -> (j p) t"), kf[:, PAST:PAST + TS])\
                    .then_inc(kf_stored, 16)
                act.wait_ge(rg_dve, 10 * j + 10)
                act.dma_start(mix_d[ds(j + NJ, 1), :, :, 0:TP].rearrange("j p s t -> (j p) s t"),
                              rstage[:, :, 0:TP]).then_inc(rnn_stored, 16)
                act.dma_start(mix_d[ds(j + NJ, 1), :, :, TP:T].rearrange("j p s t -> (j p) s t"),
                              rstage[:, :, TP + 3:LB]).then_inc(rnn_stored, 16)
                act.wait_ge(c_dve, NV * j + 2 * NV)
                act.dma_start(a["v_prompt"][:, :, ds(j, 1), :].rearrange("c p j d -> p (c j) d"),
                              vv[:, NT - 4:NT, :]).then_inc(v_stored, 16)
                act.dma_start(a["v_sample"][:, ds(j, 1), :].rearrange("p j d -> p (j d)"),
                              vv[0:TS, NT + 4, :]).then_inc(v_stored, 16)

                def exps(n, h, rows, w):
                    act.wait_ge(s_negmax, n)
                    act.activation(pr[0:rows, h, 0:w], pr[0:rows, h, 0:w], ACT.Exp, bias=nmx[0:rows, h:h + 1],
                                   accum_out=sm[0:rows, h:h + 1]).then_inc(p_ready, 1)

                def probs(n, h, rows, w):
                    act.wait_ge(t_filled, n)
                    m = min(4, (w + P - 1) // P)
                    act.activation(pt[:, h, 0:m * P], ps[:, 4, 0:m * P], ACT.Copy).then_inc(t_act, 1)

                def out_hi(n, t, w):
                    act.wait_ge(ot_filled, n)
                    act.activation(ost[:, 0, ds(t, w)], ps[:, 7, 0:w], ACT.Copy, scale=XS).then_inc(ot_hi, 1)

                un = NUNIT * j
                tn = (NT + 1) * j
                act.wait_ge(attn_stored, 16 * j + 16)
                for p in range(5):
                    w = min(BAND, P * (p + 1))
                    pw = min(BAND, P * p)
                    for h in range(2):
                        if p or h:
                            probs(un + 2 * p + h, 1 - h, P, w if h else pw)
                        exps(un + 2 * p + h + 1, h, P, w)
                        if h == 0 and p >= 2:
                            out_hi(tn + p - 1, (p - 2) * P, P)
                with nc.scalar.Fori(5, NT) as p:
                    for h in range(2):
                        probs(un + 2 * p + h, 1 - h, P, BAND)
                        exps(un + 2 * p + h + 1, h, P, BAND)
                        if h == 0:
                            out_hi(tn + p - 1, (p - 2) * P, P)
                probs(un + 2 * NT, 1, P, BAND)
                exps(un + 2 * NT + 1, 0, TS, PAST + TS)
                out_hi(tn + NT - 1, (NT - 2) * P, P)
                probs(un + 2 * NT + 1, 0, TS, PAST + TS)
                exps(un + 2 * NT + 2, 1, TS, PAST + TS)
                probs(un + 2 * NT + 2, 1, TS, PAST + TS)
                out_hi(tn + NT, (NT - 1) * P, P)
                out_hi(tn + NT + 1, TP, TS)
                act.wait_ge(ot_ready, (NT + 1) * (j + 2))
                act.dma_start(mix_d[ds(j, 1)].rearrange("j p s t -> (j p) s t"), ost).then_inc(attn_stored, 16)
            act.dma_start(a["rnn_hold"], hold_conv).then_inc(hold_stored, 16)

            act.sem_inc(d_act, 4)
            act.sem_inc(m_stored, 16)

            def merge_hi(it, q):
                f = 2 * it + q
                for i in range(3):
                    act.wait_ge(d_loaded[i], 16 * f + 16)
                    if i == 0:
                        act.wait_ge(d_filled, 20 * f + 20)
                    act.activation(dsp[:, 3 * q + i, 0], dst[:, i], ACT.Copy, scale=WS).then_inc(d_hi, 1)

            def merge_body(it, last):
                for q in range(2):
                    f = 2 * it + q
                    for n, (t, w) in enumerate(BLOCKS):
                        g, b = 5 * f + n, (5 * q + n) % 2
                        for m in range(2):
                            act.wait_ge(d_filled, 40 + 4 * g + m + 1)
                            act.activation(sig[:, b, m, 0:w], ps[:, 4 * b + m, 0:w], ACT.Sigmoid, scale=CS)\
                                .then_inc(d_act, 1)
                        if n == 0:
                            act.wait_ge(m_stored, 16 * f + 16)
                        act.wait_ge(d_step, g + 1)
                        act.activation(mstage[:, 0, t:t + w], mrg[:, b, 0:w], ACT.Copy).then_inc(d_mhi, 1)
                        if n == 1 and not (last and q == 1):
                            merge_hi(it + q, 1 - q)
                    act.wait_ge(d_mlo, 5 * f + 5)
                    act.dma_start(merged_d[ds(f, 1)].rearrange("f p s t -> (f p) s t"), mstage)\
                        .then_inc(m_stored, 16)

            merge_hi(0, 0)
            with nc.scalar.Fori(0, KT // 2 - 1) as it:
                merge_body(it, False)
            merge_body(KT // 2 - 1, True)

            for b in range(2):
                act.sem_inc(x1_stored[b], 16)
            act.wait_ge(m_stored, 16 * (KT + 1))
            with nc.scalar.Fori(0, KT // 2) as it:
                for s in range(2):
                    act.wait_ge(e_loaded[s], 16 * it + 16)
                    act.activation(wo[:, ds(2 * it + s, 1), 0, :].rearrange("p k m -> p (k m)"), est[:, s],
                                   ACT.Copy, scale=WS).then_inc(e_whi, 1)

            def square(i, b, rows):
                act.wait_ge(e_evac, i + 3)
                act.dma_start(x1_d[ds(i * P, rows), :], ex[0:rows, b]).then_inc(x1_stored[b], 16)
                act.wait_ge(e_xt, i + 1)
                act.activation(exn[0:rows, b], ex[0:rows, b], ACT.Square, accum_out=rstd[0:rows, b:b + 1])\
                    .then_inc(e_ss, 1)

            def high(i, b, rows):
                for q in range(2):
                    act.wait_ge(e_tmp, 2 * i + q + 4)
                    act.activation(hT[:, 4 * q:4 * q + 4, 0, ds(i * P, rows)],
                                   etmp[:, b, 4 * q:4 * q + 4, 0:rows], ACT.Copy).then_inc(e_hi, 1)

            def scale_rows(i, b, rows):
                act.wait_ge(e_var, i + 1)
                act.activation(rstd[0:rows, 2 + b:3 + b], rstd[0:rows, b:b + 1], ACT.Sqrt).then_inc(e_std, 1)
                act.wait_ge(e_rstd, i + 1)
                act.mul(exn[0:rows, b], ex[0:rows, b], rstd[0:rows, 4 + b:5 + b]).then_inc(e_xn, 1)

            act.wait_ge(e_split, 2 + KT)
            square(0, 0, P)
            scale_rows(0, 0, P)
            with nc.scalar.Fori(0, NT // 2 - 1) as it:
                for b in range(2):
                    i = 2 * it + 1 + b
                    square(i, 1 - b, P)
                    high(2 * it + b, b, P)
                    scale_rows(i, 1 - b, P)
            square(NT - 1, 1, P)
            high(NT - 2, 0, P)
            scale_rows(NT - 1, 1, P)
            square(NT, 0, TS)
            high(NT - 1, 1, P)
            scale_rows(NT, 0, TS)
            high(NT, 0, TS)

            act.sem_inc(f_act, 10)
            act.sem_inc(h_stored, 32)
            act.wait_ge(e_xt, NT + 3)

            def up_hi(n, s, count, free):
                act.wait_ge(f_loaded[s], 16 * count)
                if free is not None:
                    act.wait_ge(f_filled, free)
                act.activation(fsp[:, s, 0].rearrange("p k m -> p (k m)"), fst[:, s], ACT.Copy, scale=WS)\
                    .then_inc(f_hi, 1)

            def evacuate(f, s):
                act.wait_ge(f_conv, 6 * f + 3 * s + 1)
                state = col("fstate", 0, 88).rearrange("p (f c) -> p f c", c=2)[:, ds(f + NF * s, 1), :]
                act.activation(ubuf[:, TP + 2:TP + 4].rearrange("p (a c) -> p a c", a=1), state, ACT.Copy)\
                    .then_inc(f_pad, 1)
                for n, (t, w) in enumerate(BLOCKS):
                    o = 2 if t < TP else 4
                    act.wait_ge(f_filled, 10 * f + 10 + 5 * s + n + 1)
                    act.activation(ubuf[:, t + o:t + o + w], ps[:, (5 * s + n) % 8, 0:w], ACT.Copy, scale=CS)\
                        .then_inc(f_act, 1)

            def ffn_body(f, last):
                up_hi(f, 1, f + 1, 10 * f + 10)
                evacuate(f, 0)
                act.wait_ge(f_loaded[0], 16 * (2 * f + 2))
                act.activation(wd[:, ds(f, 1), 0, :].rearrange("p k m -> p (k m)"), fst[:, 0], ACT.Copy, scale=WS)\
                    .then_inc(f_hi, 1)
                if not last:
                    up_hi(f, 0, 2 * f + 3, 10 * f + 15)
                evacuate(f, 1)
                act.wait_ge(f_conv, 6 * f + 7)
                act.activation(ygate, ygate, ACT.Gelu_apprx_tanh).then_inc(f_gelu, 1)
                act.wait_ge(f_prod, f + 1)
                act.wait_ge(h_stored, 32 * f + 32)
                act.activation(hstage[:, 0, :], yval, ACT.Copy).then_inc(f_phi, 1)
                act.wait_ge(f_plo, f + 2)
                act.dma_start(hid_d[ds(f, 1), :, :, 0:TP].rearrange("f p s t -> (f p) s t"), hstage[:, :, 0:TP])\
                    .then_inc(h_stored, 16)
                act.dma_start(hid_d[ds(f, 1), :, :, TP:T].rearrange("f p s t -> (f p) s t"),
                              hstage[:, :, TP + 2:LF]).then_inc(h_stored, 16)

            up_hi(0, 0, 1, None)
            act.activation(ubuf[:, 0:2], ident[:, 0:2], ACT.Copy, scale=0.0).then_inc(f_pad, 1)
            with nc.scalar.Fori(0, NF - 1) as f:
                ffn_body(f, False)
            ffn_body(NF - 1, True)
            act.dma_start(a["ffn_hold"], fhold).then_inc(hold_stored, 16)

            for b in range(2):
                act.sem_inc(y_stored[b], 16)

            def finish(i, b, rows, out):
                act.wait_ge(g_evac, i + 3)
                act.activation(ps[0:rows, 4 + 2 * b:6 + 2 * b, :].rearrange("p b n -> p (b n)"), gx[0:rows, b],
                               ACT.Square, accum_out=rstd[0:rows, b:b + 1]).then_inc(g_ss, 1)
                act.wait_ge(g_var, i + 1)
                act.activation(rstd[0:rows, 2 + b:3 + b], rstd[0:rows, b:b + 1], ACT.Sqrt).then_inc(g_std, 1)
                act.wait_ge(g_y, i + 1)
                act.dma_start(out, gx[0:rows, b]).then_inc(y_stored[b], 16)

            with nc.scalar.Fori(0, NT // 2) as it:
                for b in range(2):
                    finish(2 * it + b, b, P, a["y_prompt"][ds(2 * P * it + b * P, P), :])
            finish(NT, 0, TS, a["y_sample"])
            act.wait_ge(hold_stored, 32)
            act.wait_ge(y_stored[0], 16 * (NT // 2 + 2))
            act.wait_ge(y_stored[1], 16 * (NT // 2 + 1))

        @block.vector
        def _(dve):
            done = [0]

            def chain(ins):
                done[0] += 1
                ins.then_inc(dve_seq, 1)
                dve.wait_ge(dve_seq, done[0])

            dve.wait_ge(tab_loaded, 16)
            dve.tensor_copy(tabr[0:8, 0:383], tab[0:8, 0:1].to_broadcast([8, 383])).then_inc(tab_ready, 1)
            dve.tensor_copy(tabr[0:8, 383:767], tab[0:8, 0:384]).then_inc(tab_ready, 1)
            dve.wait_ge(silu_sig, 1)
            dve.tensor_tensor(cs, col("c", 0, 16), sgc, ALU.mult).then_inc(silu_ready, 1)
            z, s1, s2, acc, lp = (small[:, 4 * i:4 * i + 4] for i in (1, 2, 3, 4, 5))
            dve.wait_ge(sp_a, 2)
            chain(dve.tensor_scalar(s1, z, 2.0, None, ALU.add))
            chain(dve.reciprocal(s2, s1))
            chain(dve.tensor_tensor(s1, z, s2, ALU.mult))
            chain(dve.tensor_tensor(s2, s1, s1, ALU.mult))
            chain(dve.tensor_scalar(acc, s2, 1 / 17.0, 1 / 15.0, ALU.mult, ALU.add))
            for k in (13, 11, 9, 7, 5, 3, 1):
                chain(dve.tensor_tensor(acc, acc, s2, ALU.mult))
                chain(dve.tensor_scalar(acc, acc, 1.0 / k, None, ALU.add))
            chain(dve.scalar_tensor_tensor(lp, acc, 2.0, s1, ALU.mult, ALU.mult))
            chain(dve.tensor_scalar(acc, col("lam", 0, 4), -1.0, 0.0, ALU.mult, ALU.max))
            chain(dve.tensor_tensor(lp, lp, acc, ALU.add))
            dve.tensor_scalar(sp8, lp, 8.0, None, ALU.mult).then_inc(sp_v, 1)

            dve.wait_ge(ss_ready, NT + 1)
            dve.tensor_scalar(rstd[:, 0:NT], rstd[:, 0:NT], 1.0 / D, EPS, ALU.mult, ALU.add)
            dve.tensor_scalar(rstd[0:TS, NT:NT + 1], rstd[0:TS, NT:NT + 1], 1.0 / D, EPS, ALU.mult, ALU.add)
            dve.memset(rstd[TS:P, NT:NT + 1], 1.0).then_inc(var_ready, 1)
            dve.wait_ge(std_ready, 1)
            dve.reciprocal(rstd[:, 0:NT + 1], rstd[:, 0:NT + 1]).then_inc(rstd_ready, 1)

            def coefficients(m):
                c = COLS["mod_b"] + 24 * m
                for s in range(2):
                    chain(dve.tensor_tensor(modv[:, m, :, s], ps[:, 6, 48 * m:48 * m + 48].rearrange(
                        "p (f s) -> p f s", s=2)[:, :, s], par[:, c:c + 24], ALU.add))
                g = col("g_mix" if m == 0 else "g_ffn", 0, KT)
                for s in range(2):
                    chain(dve.scalar_tensor_tensor(coefv[:, m, 0, s], modv[:, m, KT:2 * KT, s], 1.0, g,
                                                   ALU.add, ALU.mult))
                    chain(dve.tensor_scalar(coefv[:, m, 0, s], coefv[:, m, 0, s], XS, None, ALU.mult))
                    chain(dve.tensor_scalar(coefv[:, m, 1, s], modv[:, m, 0:KT, s], XS, None, ALU.mult))

            dve.sem_inc(tmp_ready, 3)
            dve.wait_ge(mod_filled, 4 + 48)
            coefficients(0)
            coefficients(1)
            for m in range(2):
                for s in range(2):
                    i = dve.tensor_copy(gcols[:, 16 * m + 8 * s:16 * m + 8 * s + 8], modv[:, m, 16:24, s])
            i.then_inc(gcols_ready, 1)

            def modulate(i, rows, half, m, src):
                for q in range(2):
                    if q == 0:
                        dve.wait_ge(xT_filled, i + 3)
                    for k in range(4 * q, 4 * q + 4):
                        ins = dve.tensor_scalar(tmp[:, half, k, 0:rows],
                                                ps[:, 2 * half + q, (k % 4) * P:(k % 4) * P + rows],
                                                coefv[:, m, 0, src, k:k + 1], coefv[:, m, 1, src, k:k + 1],
                                                ALU.mult, ALU.add)
                    ins.then_inc(tmp_ready, 1)
                for q in range(2):
                    dve.wait_ge(hi_ready, 2 * i + q + 1)
                    k = slice(4 * q, 4 * q + 4)
                    dve.tensor_tensor(hT[:, k, 1, ds(i * P, rows)], tmp[:, half, k, 0:rows],
                                      hT[:, k, 0, ds(i * P, rows)], ALU.subtract).then_inc(hT_ready, 1)

            with nc.vector.Fori(0, NT // 2) as it:
                for b in range(2):
                    modulate(2 * it + b, P, b, 0, 0)
            modulate(NT, TS, 0, 0, 1)

            dve.sem_inc(c_dve, NV)
            dve.sem_inc(w_split, 5)
            dve.sem_inc(ot_ready, NT + 1)
            dve.wait_ge(gate_rows_stored, 16)
            dve.wait_ge(gap_ready, 2)
            with nc.vector.Fori(0, NJ) as j:
                def split_lo(i):
                    s = UNITS[i][1]
                    dve.wait_ge(w_hi, 5 * j + i + 1)
                    dve.scalar_tensor_tensor(wsp[:, s, 1], wst[:, s], WS, wsp[:, s, 0], ALU.mult, ALU.subtract)\
                        .then_inc(w_split, 1)

                n_chain = [0]

                def step(ins):
                    n_chain[0] += 1
                    ins.then_inc(rg_dve, 1)
                    return n_chain[0]

                def after(n):
                    dve.wait_ge(rg_dve, 10 * j + n)

                split_lo(0)
                split_lo(1)
                dve.wait_ge(c_act, NA * j + NA + 5)
                dve.wait_ge(rg_act, 6 * j + 2)
                cw = col("cw", 0, 16).rearrange("p (j w) -> p j w", w=4)
                w_at = lambda n: cw[:, ds(j, 1), n:n + 1].rearrange("p j w -> p (j w)")
                cb, sp8j = col("cb", 0, 4)[:, ds(j, 1)], sp8[:, ds(j, 1)]
                for g, b in enumerate(("ba", "bx")):
                    dve.tensor_copy(gbias[:, g:g + 1], col(b, 0, 4)[:, ds(j, 1)])
                dve.tensor_copy(holdv[:, ds(j, 1), 0:3].rearrange("p j c -> p (j c)"), bufA[:, TP:TP + 3])
                dve.tensor_copy(holdv[:, ds(j, 1), 3:6].rearrange("p j c -> p (j c)"),
                                bufA[:, TP + 3 + TS:TP + 6 + TS])
                dve.tensor_scalar(bufX, bufA[:, 0:LB], w_at(0), cb, ALU.mult, ALU.add).then_inc(xc_ready, 1)
                for n in range(1, 4):
                    dve.wait_ge(xc_ready, 4 * j + n)
                    dve.scalar_tensor_tensor(bufX, bufA[:, n:n + LB], w_at(n), bufX, ALU.mult, ALU.add)\
                        .then_inc(xc_ready, 1)
                split_lo(2)
                split_lo(3)

                def q_lo(n):
                    t, w = BLOCKS[n]
                    u = U_Q + n
                    dve.wait_ge(c_hi, 11 * j + n + 1)
                    for h in range(2):
                        own, other = slice(64 * h, 64 * h + 64), slice(64 - 64 * h, 128 - 64 * h)
                        ins = dve.scalar_tensor_tensor(qs[other, h, t:t + w], ps[own, u % 8, 0:w], CS * HD ** -0.5,
                                                       qs[own, h, t:t + w], ALU.mult, ALU.subtract)
                    ins.then_inc(c_dve, 1)

                def k_lo(n):
                    if n < 5:
                        t, w = BLOCKS[n]
                        kt, u, sc = (t if t < TP else TP + PAST), U_K + n, CS
                    else:
                        kt, w, u, sc = TP, PAST, U_KC, 1.0
                    dve.wait_ge(c_hi, 11 * j + 5 + n + 1)
                    for h in range(2):
                        own = slice(64 * h, 64 * h + 64)
                        ins = dve.scalar_tensor_tensor(kll[own, h, kt:kt + w], ps[own, u % 8, 0:w], sc,
                                                       khh[own, h, kt:kt + w], ALU.mult, ALU.subtract)
                    ins.then_inc(c_dve, 1)
                    dve.wait_ge(c_dve, NV * j + NV + 5 + n + 1)
                    for h in range(2):
                        own, other = slice(64 * h, 64 * h + 64), slice(64 - 64 * h, 128 - 64 * h)
                        dve.tensor_copy(khh[other, h, kt:kt + w], khh[own, h, kt:kt + w])
                        ins = dve.tensor_copy(kll[other, h, kt:kt + w], kll[own, h, kt:kt + w])
                    ins.then_inc(kdup, 1)

                def v_out(b):
                    u = U_V + b
                    dve.wait_ge(c_filled, NU * j + NU + u + 1)
                    if b < 4:
                        dve.tensor_scalar(vv[:, 4 * b:4 * b + 4, :],
                                          ps[:, u % 8, :].rearrange("p (i d) -> p i d", d=P), CS, None, ALU.mult)\
                            .then_inc(c_dve, 1)
                    else:
                        dve.tensor_scalar(vv[0:TS, NT + 4, :], ps[0:TS, u % 8, 0:P], CS, None, ALU.mult)\
                            .then_inc(c_dve, 1)

                for n in range(5):
                    q_lo(n)
                split_lo(4)
                dve.wait_ge(c_act, NA * j + NA + 20)
                step(dve.memset(bufA[:, TP:TP + 3], 0.0))
                after(1)
                step(dve.tensor_scalar(bufA[:, 0:LB], bufA[:, 0:LB], sp8j, None, ALU.mult))
                k_lo(0)
                k_lo(1)
                dve.wait_ge(rg_act, 6 * j + 3)
                dve.wait_ge(rnn_stored, 32 * j + 32)
                step(dve.tensor_scalar(bufR, bufT, 1.0, None, ALU.add))
                after(3)
                step(dve.reciprocal(bufR, bufR))
                after(4)
                step(dve.scalar_tensor_tensor(bufT, bufT, 2.0, bufR, ALU.mult, ALU.mult))
                k_lo(2)
                k_lo(3)
                step(dve.tensor_tensor(bufI, bufI, bufX, ALU.mult))
                k_lo(4)
                k_lo(5)
                dve.wait_ge(rg_act, 6 * j + 5)
                after(6)
                step(dve.tensor_tensor(bufI, bufI, bufT, ALU.mult))
                dve.wait_ge(v_stored, 32 * j + 32)
                v_out(0)
                after(7)
                dve.tensor_tensor_scan(bufX[:, 0:TP], bufA[:, 0:TP], bufI[:, 0:TP], 0.0, ALU.mult, ALU.add)
                step(dve.tensor_tensor_scan(bufX[:, TP + 3:LB], bufA[:, TP + 3:LB], bufI[:, TP + 3:LB],
                                            col("h0", 0, 4)[:, ds(j, 1)], ALU.mult, ALU.add))
                v_out(1)
                after(8)
                dve.tensor_copy(holdv[:, ds(j, 1), 6:7].rearrange("p j c -> p (j c)"), bufX[:, TP - 1:TP])
                dve.tensor_copy(holdv[:, ds(j, 1), 7:8].rearrange("p j c -> p (j c)"), bufX[:, LB - 1:LB])\
                    .then_inc(held, 1)
                dve.wait_ge(held, j + 1)
                step(dve.tensor_tensor(bufX, bufX, bufG, ALU.mult))
                v_out(2)
                dve.wait_ge(rg_act, 6 * j + 6)
                after(9)
                step(dve.scalar_tensor_tensor(rstage[:, 1, :], bufX, XS, rstage[:, 0, :], ALU.mult, ALU.subtract))
                v_out(3)
                v_out(4)
                dve.wait_ge(aux_loaded, 16 * j + 16)
                dve.memset(bias[0:64, :, BAND - 64:BAND], NEG)
                dve.memset(bias[64:128, :, 0:64], NEG).then_inc(bias_masked, 1)
                dve.wait_ge(bias_masked, j + 1)

                def scores(n, h, rows, w, b0, old):
                    dve.wait_ge(s_filled, n)
                    if old is not None:
                        dve.wait_ge(t_filled, old)
                    if w > 512:
                        src = ps[0:rows, 2 * h:2 * h + 2, :].rearrange("p b n -> p (b n)")[:, 0:w]
                    else:
                        src = ps[0:rows, 2 * h, 0:w]
                    dve.memset(mark, 0.0)
                    dve.tensor_tensor_reduce(pr[0:rows, h, 0:w], src, bias[0:rows, h, b0:b0 + w], 1.0, -3.0e38,
                                             ALU.add, ALU.max, mx[0:rows, h:h + 1]).then_inc(s_added, 1)
                    dve.wait_ge(s_added, n)
                    dve.tensor_scalar(nmx[0:rows, h:h + 1], mx[0:rows, h:h + 1], -1.0, None, ALU.mult)\
                        .then_inc(s_negmax, 1)

                def probs(n, h, rows, w):
                    dve.wait_ge(p_ready, n)
                    dve.reciprocal(rs[0:rows, h:h + 1], sm[0:rows, h:h + 1]).then_inc(r_ready, 1)
                    if w > 512:
                        k = min(P, w - 512)
                        dve.wait_ge(t_filled, n)
                        dve.tensor_copy(pt[0:k, h, 4 * P:5 * P], ps[0:k, 5, 0:P]).then_inc(t_dve, 1)

                def out_n(n, h, rows, ot):
                    dve.wait_ge(o_filled, n)
                    dve.wait_ge(r_ready, n)
                    if ot is not None:
                        dve.wait_ge(ot_filled, ot)
                    dve.tensor_scalar(osb[0:rows, 64 * h:64 * h + 64], ps[0:rows, 6, 64 * h:64 * h + 64],
                                      rs[0:rows, h:h + 1], None, ALU.mult).then_inc(o_ready, 1)

                def out_lo(n, t, w):
                    dve.wait_ge(ot_hi, n)
                    dve.scalar_tensor_tensor(ost[:, 1, ds(t, w)], ps[:, 7, 0:w], XS, ost[:, 0, ds(t, w)],
                                             ALU.mult, ALU.subtract).then_inc(ot_ready, 1)

                un = NUNIT * j
                tn = (NT + 1) * j
                for p in range(5):
                    w, pw = min(BAND, P * (p + 1)), min(BAND, P * p)
                    for h in range(2):
                        scores(un + 2 * p + h + 1, h, P, w, BAND - w, un + 2 * p + h - 1 if p else None)
                        if p or h:
                            probs(un + 2 * p + h, 1 - h, P, w if h else pw)
                        if p:
                            out_n(un + 2 * p + h - 1, h, P, tn + p - 1 if p >= 2 and h == 0 else None)
                        if h == 0 and p >= 2:
                            out_lo(tn + p - 1, (p - 2) * P, P)
                with nc.vector.Fori(5, NT) as p:
                    for h in range(2):
                        scores(un + 2 * p + h + 1, h, P, BAND, 0, un + 2 * p + h - 1)
                        probs(un + 2 * p + h, 1 - h, P, BAND)
                        out_n(un + 2 * p + h - 1, h, P, tn + p - 1 if h == 0 else None)
                        if h == 0:
                            out_lo(tn + p - 1, (p - 2) * P, P)
                scores(un + 2 * NT + 1, 0, TS, PAST + TS, 0, un + 2 * NT - 1)
                probs(un + 2 * NT, 1, P, BAND)
                out_n(un + 2 * NT - 1, 0, P, tn + NT - 1)
                out_lo(tn + NT - 1, (NT - 2) * P, P)
                scores(un + 2 * NT + 2, 1, TS, PAST + TS, 0, un + 2 * NT)
                probs(un + 2 * NT + 1, 0, TS, PAST + TS)
                out_n(un + 2 * NT, 1, P, None)
                dve.wait_ge(o_ready, un + 2 * NT)
                probs(un + 2 * NT + 2, 1, TS, PAST + TS)
                out_lo(tn + NT, (NT - 1) * P, P)
                out_n(un + 2 * NT + 1, 0, TS, tn + NT)
                out_n(un + 2 * NT + 2, 1, TS, None)
                out_lo(tn + NT + 1, TP, TS)

            dve.sem_inc(d_dve, 4)
            dve.sem_inc(d_split, 3)

            def merge_lo(it, q):
                for i in range(3):
                    dve.wait_ge(d_hi, 6 * it + 3 * q + i + 1)
                    dve.scalar_tensor_tensor(dsp[:, 3 * q + i, 1], dst[:, i], WS, dsp[:, 3 * q + i, 0],
                                             ALU.mult, ALU.subtract).then_inc(d_split, 1)

            def merge_body(it, last):
                for q in range(2):
                    for n, (t, w) in enumerate(BLOCKS):
                        g, b = 10 * it + 5 * q + n, (5 * q + n) % 2
                        for m in range(2):
                            dve.wait_ge(d_filled, 40 + 4 * g + m + 3)
                            dve.wait_ge(d_act, 4 + 2 * g + m + 1)
                            dve.scalar_tensor_tensor(prod[:, m, 0:w], ps[:, 4 * b + 2 + m, 0:w], 1.0 / WS,
                                                     sig[:, b, m, 0:w], ALU.mult, ALU.mult).then_inc(d_dve, 1)
                        dve.wait_ge(d_dve, 4 + 2 * g + 2)
                        dve.tensor_tensor(mrg[:, b, 0:w], prod[:, 0, 0:w], prod[:, 1, 0:w], ALU.add)\
                            .then_inc(d_step, 1)
                        dve.wait_ge(d_mhi, g + 1)
                        dve.tensor_tensor(mstage[:, 1, t:t + w], mrg[:, b, 0:w], mstage[:, 0, t:t + w],
                                          ALU.subtract).then_inc(d_mlo, 1)
                        if n == 1 and not (last and q == 1):
                            merge_lo(it + q, 1 - q)

            merge_lo(0, 0)
            with nc.vector.Fori(0, KT // 2 - 1) as it:
                merge_body(it, False)
            merge_body(KT // 2 - 1, True)

            dve.sem_inc(e_split, 2)
            dve.sem_inc(e_evac, 2)
            dve.sem_inc(e_tmp, 3)
            with nc.vector.Fori(0, KT // 2) as it:
                for s in range(2):
                    dve.wait_ge(e_whi, 2 * it + s + 1)
                    dve.scalar_tensor_tensor(wo[:, ds(2 * it + s, 1), 1, :].rearrange("p k m -> p (k m)"), est[:, s],
                                             WS, wo[:, ds(2 * it + s, 1), 0, :].rearrange("p k m -> p (k m)"),
                                             ALU.mult, ALU.subtract).then_inc(e_split, 1)

            def residual(i, b, rows, src, nx, sems, xbuf, gates):
                filled, loaded, gated, evac = sems
                dve.wait_ge(filled, i + 1)
                out = ps[0:rows, 2 * b:2 * b + 2, :].rearrange("p b n -> p (b n)")
                dve.scalar_tensor_tensor(out, out, CS, gates[0:rows, src, :], ALU.mult, ALU.mult).then_inc(gated, 1)
                dve.wait_ge(loaded[b], 16 * nx)
                dve.wait_ge(gated, i + 1)
                dve.tensor_tensor(xbuf[0:rows, b], out, xbuf[0:rows, b], ALU.add).then_inc(evac, 1)

            def variance(i, b, rows, sems):
                ss, var, std, rst = sems
                dve.wait_ge(ss, i + 1)
                dve.tensor_scalar(rstd[0:rows, b:b + 1], rstd[0:rows, b:b + 1], 1.0 / D, EPS, ALU.mult, ALU.add)\
                    .then_inc(var, 1)
                dve.wait_ge(std, i + 1)
                dve.reciprocal(rstd[0:rows, 4 + b:5 + b], rstd[0:rows, 2 + b:3 + b]).then_inc(rst, 1)

            def modulate2(i, b, rows, src):
                for q in range(2):
                    if q == 0:
                        dve.wait_ge(e_xt, i + 3)
                    for k in range(4 * q, 4 * q + 4):
                        ins = dve.tensor_scalar(etmp[:, b, k, 0:rows],
                                                ps[:, 4 + 2 * b + q, (k % 4) * P:(k % 4) * P + rows],
                                                coefv[:, 1, 0, src, k:k + 1], coefv[:, 1, 1, src, k:k + 1],
                                                ALU.mult, ALU.add)
                    ins.then_inc(e_tmp, 1)

            def low2(i, b, rows):
                for q in range(2):
                    dve.wait_ge(e_hi, 2 * i + q + 1)
                    k = slice(4 * q, 4 * q + 4)
                    dve.tensor_tensor(hT[:, k, 1, ds(i * P, rows)], etmp[:, b, k, 0:rows],
                                      hT[:, k, 0, ds(i * P, rows)], ALU.subtract).then_inc(e_hT, 1)

            E1, E2 = (e_filled, ex_loaded, e_gated, e_evac), (e_ss, e_var, e_std, e_rstd)
            dve.wait_ge(gate1_loaded, 32)
            residual(0, 0, P, 0, 1, E1, ex, gate1)
            variance(0, 0, P, E2)
            with nc.vector.Fori(0, NT // 2 - 1) as it:
                for b in range(2):
                    i = 2 * it + 1 + b
                    residual(i, 1 - b, P, 0, it + 1 + b, E1, ex, gate1)
                    modulate2(2 * it + b, b, P, 0)
                    variance(i, 1 - b, P, E2)
                    low2(2 * it + b, b, P)
            residual(NT - 1, 1, P, 0, NT // 2, E1, ex, gate1)
            modulate2(NT - 2, 0, P, 0)
            variance(NT - 1, 1, P, E2)
            low2(NT - 2, 0, P)
            residual(NT, 0, TS, 1, NT // 2 + 1, E1, ex, gate1)
            modulate2(NT - 1, 1, P, 0)
            variance(NT, 0, TS, E2)
            low2(NT - 1, 1, P)
            modulate2(NT, 0, TS, 1)
            low2(NT, 0, TS)

            dve.sem_inc(f_split, 3)
            dve.sem_inc(f_conv, 1)

            def up_lo(n, s):
                dve.wait_ge(f_hi, n)
                dve.scalar_tensor_tensor(fsp[:, s, 1].rearrange("p k m -> p (k m)"), fst[:, s], WS,
                                         fsp[:, s, 0].rearrange("p k m -> p (k m)"), ALU.mult, ALU.subtract)\
                    .then_inc(f_split, 1)

            def ffn_conv(f, s, out):
                dve.wait_ge(f_act, 10 * f + 10 + 5 * s + 5)
                dve.wait_ge(f_pad, 2 * f + s + 2)
                w3 = col("fw", 0, 132).rearrange("p (f c) -> p f c", c=3)[:, ds(f + NF * s, 1), :]
                tap = lambda n: w3[:, :, n:n + 1].rearrange("p a c -> p (a c)")
                fb = col("fb", 0, 44)[:, ds(f + NF * s, 1)]
                hold = fholdv[:, ds(f + NF * s, 1), :].rearrange("p f c -> p (f c)")
                dve.tensor_copy(hold[:, 0:2], ubuf[:, TP:TP + 2])
                dve.tensor_copy(hold[:, 2:4], ubuf[:, LF:LF + 2])
                dve.tensor_scalar(out, ubuf[:, 0:LF], tap(0), fb, ALU.mult, ALU.add).then_inc(f_conv, 1)
                for n in (1, 2):
                    dve.wait_ge(f_conv, 6 * f + 3 * s + n + 1)
                    dve.scalar_tensor_tensor(out, ubuf[:, n:n + LF], tap(n), out, ALU.mult, ALU.add)\
                        .then_inc(f_conv, 1)

            def ffn_body(f, last):
                up_lo(3 * f + 2, 1)
                dve.wait_ge(f_plo, f + 1)
                ffn_conv(f, 0, yval)
                dve.wait_ge(f_hi, 3 * f + 3)
                dve.scalar_tensor_tensor(wd[:, ds(f, 1), 1, :].rearrange("p k m -> p (k m)"), fst[:, 0], WS,
                                         wd[:, ds(f, 1), 0, :].rearrange("p k m -> p (k m)"),
                                         ALU.mult, ALU.subtract).then_inc(f_split, 1)
                if not last:
                    up_lo(3 * f + 4, 0)
                ffn_conv(f, 1, ygate)
                dve.wait_ge(f_gelu, f + 1)
                dve.scalar_tensor_tensor(yval, yval, XS, ygate, ALU.mult, ALU.mult).then_inc(f_prod, 1)
                dve.wait_ge(f_phi, f + 1)
                dve.tensor_tensor(hstage[:, 1, :], yval, hstage[:, 0, :], ALU.subtract).then_inc(f_plo, 1)

            up_lo(1, 0)
            dve.sem_inc(f_plo, 1)
            with nc.vector.Fori(0, NF - 1) as f:
                ffn_body(f, False)
            ffn_body(NF - 1, True)

            dve.sem_inc(g_evac, 2)
            G1, G2 = (g_filled, gx_loaded, g_gated, g_evac), (g_ss, g_var, g_std, g_rstd)

            def finish(i, b, rows, src, nx):
                residual(i, b, rows, src, nx, G1, gx, gate2)
                variance(i, b, rows, G2)
                dve.wait_ge(g_rstd, i + 1)
                dve.scalar_tensor_tensor(gx[0:rows, b], gx[0:rows, b], rstd[0:rows, 4 + b:5 + b], gfin[0:rows, :],
                                         ALU.mult, ALU.mult).then_inc(g_y, 1)

            dve.wait_ge(rows_loaded, 48)
            with nc.vector.Fori(0, NT // 2) as it:
                for b in range(2):
                    finish(2 * it + b, b, P, 0, it + 1)
            finish(NT, 0, TS, 1, NT // 2 + 1)

        @block.tensor
        def _(pe):
            pe.sem_inc(mod_filled, 4)
            pe.wait_ge(silu_ready, 1)
            with nc.tensor.Fori(0, 12) as it:
                for s in range(4):
                    pe.wait_ge(mw_loaded[s], 16 * it + 16)
                    for k in range(KT):
                        mm = pe.matmul(ps[:, 6, ds(8 * it + 2 * s, 2)], mw[:, s, k, :], csv[:, k, :],
                                       start=(k == 0), stop=(k == KT - 1))
                    mm.then_inc(mod_filled, 1)
            pe.wait_ge(ident_ready, 2)
            pe.sem_inc(xT_filled, 2)

            def transposes(i, rows, half, free):
                pe.wait_ge(xn_ready, i + 1)
                if free is not None:
                    pe.wait_ge(tmp_ready, free)
                for k in range(KT):
                    mm = pe.transpose(ps[:, 2 * half + k // 4, (k % 4) * P:(k % 4) * P + rows],
                                      xn[0:rows, half, k * P:(k + 1) * P], ident[0:rows, 0:rows])
                mm.then_inc(xT_filled, 1)

            with nc.tensor.Fori(0, NT // 2) as it:
                for b in range(2):
                    transposes(2 * it + b, P, b, 4 * it + 2 * b + 1)
            transposes(NT, TS, 0, 2 * NT + 1)
            pe.wait_ge(gcols_ready, 1)
            pe.transpose(ps[0:32, 5, 0:P], gcols, ident).then_inc(grow_filled, 1)

            pe.sem_inc(c_filled, NU)
            pe.wait_ge(hT_ready, 2 * (NT + 1))
            pe.wait_ge(grow_ready, 1)
            with nc.tensor.Fori(0, NJ) as j:
                def bank(u):
                    if u >= 8:
                        e, n = drained_before(u - 8)
                        if e == "A":
                            pe.wait_ge(c_act, NA * j + NA + n)
                        else:
                            pe.wait_ge(c_dve, NV * j + NV + n)
                    return ps[:, u % 8, :]

                def unit(u0, s):
                    for n, (t, w) in enumerate(BLOCKS):
                        out = bank(u0 + n)
                        for k in range(KT):
                            for m, (wp, hp) in enumerate(PASSES):
                                mm = pe.matmul(out[:, 0:w], wsp[:, s, wp, k, :], hT[:, k, hp, t:t + w],
                                               start=(k == 0 and m == 0), stop=(k == KT - 1 and m == 2))
                        mm.then_inc(c_filled, 1)

                pe.wait_ge(ot_ready, (NT + 1) * (j + 1))
                pe.wait_ge(w_split, 5 * j + 6)
                unit(U_RX, 0)
                pe.wait_ge(w_split, 5 * j + 7)
                unit(U_RG, 1)
                pe.wait_ge(w_split, 5 * j + 8)
                unit(U_Q, 0)
                pe.wait_ge(xc_ready, 4 * j + 4)
                pe.wait_ge(gw_loaded, 32 * j + 32)
                for n, (t, w) in enumerate(BLOCKS):
                    o = 0 if t < TP else 3
                    for g in range(2):
                        out = bank(U_G + 2 * n + g)
                        pe.matmul(out[:, 0:w], gw[:, g, :], bufX[:, t + o:t + o + w], start=True, stop=True)\
                            .then_inc(c_filled, 1)
                pe.wait_ge(w_split, 5 * j + 9)
                unit(U_K, 1)
                pe.wait_ge(kc_loaded, 16 * j + 16)
                out = bank(U_KC)
                for c in range(4):
                    mm = pe.transpose(out[:, c * P:(c + 1) * P], kc[:, c, :], ident)
                mm.then_inc(c_filled, 1)
                pe.wait_ge(w_split, 5 * j + 10)
                for i in range(NT + 1):
                    rows = P if i < NT else TS
                    if i % 4 == 0:
                        out = bank(U_V + i // 4)
                    for k in range(KT):
                        for m, (wp, hp) in enumerate(PASSES):
                            mm = pe.matmul(out[0:rows, (i % 4) * P:(i % 4) * P + P],
                                           hT[:, k, hp, i * P:i * P + rows], wsp[:, 0, wp, k, :],
                                           start=(k == 0 and m == 0), stop=(k == KT - 1 and m == 2))
                    if i % 4 == 3 or i == NT:
                        mm.then_inc(c_filled, 1)

                def scores(n, h, q0, rows, k0, w):
                    if n is not None:
                        pe.wait_ge(s_added, n)
                    for b, c in ((0, min(w, 512)), (1, w - 512)):
                        if c <= 0:
                            continue
                        for m, kk in enumerate((khh, kll)):
                            mm = pe.matmul(ps[0:rows, 2 * h + b, 0:c], qs[:, h, ds(q0, rows)],
                                           kk[:, h, ds(k0 + 512 * b, c)], start=(m == 0), stop=(m == 1))
                    mm.then_inc(s_filled, 1)

                def probs(n, h, rows, w, ta, td):
                    pe.wait_ge(p_ready, n)
                    if ta is not None:
                        pe.wait_ge(t_act, ta)
                    if td is not None:
                        pe.wait_ge(t_dve, td)
                    for c in range((w + P - 1) // P):
                        k = min(P, w - c * P)
                        mm = pe.transpose(ps[0:k, 4 + c // 4, (c % 4) * P:(c % 4) * P + P],
                                          pr[:, h, c * P:c * P + k], ident)
                    mm.then_inc(t_filled, 1)

                def outs(n, h, rows, v0, w, td, on):
                    pe.wait_ge(t_act, n)
                    if td is not None:
                        pe.wait_ge(t_dve, td)
                    if on is not None:
                        pe.wait_ge(o_ready, on)
                    nk = (w + P - 1) // P
                    for c in range(nk):
                        k = min(P, w - c * P)
                        mm = pe.matmul(ps[0:rows, 6, 64 * h:64 * h + 64], pt[0:k, h, c * P:c * P + rows],
                                       vv[0:k, ds(v0 + c, 1), 64 * h:64 * h + 64].rearrange("p a d -> p (a d)"),
                                       start=(c == 0), stop=(c == nk - 1))
                    mm.then_inc(o_filled, 1)

                def out_t(n, rows, hi):
                    pe.wait_ge(o_ready, 2 * n)
                    if hi is not None:
                        pe.wait_ge(ot_ready, hi)
                    pe.transpose(ps[:, 7, 0:P], osb, ident).then_inc(ot_filled, 1)

                un = NUNIT * j
                tn = (NT + 1) * j
                full = 2 * (NT - 4) + 2
                tdn = full * j
                pe.wait_ge(kdup, 6 * j + 6)
                pe.wait_ge(c_dve, NV * j + 2 * NV)
                pe.wait_ge(c_act, NA * j + 2 * NA)
                pe.wait_ge(v_loaded, 16 * j + 16)

                def td_of(unit):
                    n = max(0, unit - 7)
                    return tdn + n if n > 0 else None

                for p in range(5):
                    w, pw = min(BAND, P * (p + 1)), min(BAND, P * p)
                    k0 = 0
                    for h in range(2):
                        i = 2 * p + h
                        scores(un + i - 1 if i >= 2 else None, h, p * P, P, k0, w)
                        if h == 0 and p >= 2:
                            out_t(tn + p - 1, P, tn + p + NT - 1 if p > 2 else None)
                        if i >= 1:
                            probs(un + i, 1 - h, P, w if h else pw, un + i - 1 if i >= 2 else None, td_of(i - 2))
                        if i >= 2:
                            outs(un + i - 1, h, P, 0, pw, td_of(i - 2), un + i - 2 if i >= 3 else None)
                with nc.tensor.Fori(5, NT) as p:
                    for h in range(2):
                        i = 2 * p + h
                        scores(un + i - 1, h, p * P, P, (p - 4) * P, BAND)
                        if h == 0:
                            out_t(tn + p - 1, P, tn + p + NT - 1)
                        probs(un + i, 1 - h, P, BAND, un + i - 1, tdn + i - 9)
                        outs(un + i - 1, h, P, p - 5, BAND, tdn + i - 9, un + i - 2)
                i = 2 * NT
                ws = PAST + TS
                scores(un + i - 1, 0, TP, TS, TP, ws)
                out_t(tn + NT - 1, P, tn + 2 * NT - 1)
                probs(un + i, 1, P, BAND, un + i - 1, tdn + i - 9)
                outs(un + i - 1, 0, P, NT - 5, BAND, tdn + i - 9, un + i - 2)
                i += 1
                scores(un + i - 1, 1, TP, TS, TP, ws)
                probs(un + i, 0, TS, ws, un + i - 1, tdn + i - 9)
                outs(un + i - 1, 1, P, NT - 5, BAND, tdn + i - 9, un + i - 2)
                i += 1
                probs(un + i, 1, TS, ws, un + i - 1, tdn + i - 9)
                out_t(tn + NT, P, tn + 2 * NT)
                outs(un + i - 1, 0, TS, NT, ws, tdn + i - 9, un + i - 2)
                i += 1
                outs(un + i - 1, 1, TS, NT, ws, tdn + i - 9, un + i - 2)
                out_t(tn + NT + 1, TS, tn + 2 * NT + 1)


            pe.sem_inc(d_filled, 40)
            pe.wait_ge(ot_ready, (NT + 1) * (NJ + 1))

            def product(out, w, k0, k1, wt, act_t, t, sem_):
                for k in range(k0, k1):
                    for m, (wp, hp) in enumerate(PASSES):
                        mm = pe.matmul(out, wt[:, wp, k, :], act_t[:, k, hp, t:t + w],
                                       start=(k == k0 and m == 0), stop=(k == k1 - 1 and m == 2))
                mm.then_inc(sem_, 1)

            with nc.tensor.Fori(0, KT // 2) as it:
                for q in range(2):
                    pe.wait_ge(d_split, 6 * it + 3 * q + 6)
                    for n, (t, w) in enumerate(BLOCKS):
                        g, b = 10 * it + 5 * q + n, (5 * q + n) % 2
                        pe.wait_ge(d_act, 2 * g + 2)
                        pe.wait_ge(d_dve, 2 * g + 2)
                        for m in range(2):
                            product(ps[:, 4 * b + m, 0:w], w, 0, KT, dsp[:, 3 * q + m], hT, t, d_filled)
                        pe.wait_ge(mix_loaded, 16 * KT)
                        for m in range(2):
                            product(ps[:, 4 * b + 2 + m, 0:w], w, 4 * m, 4 * m + 4, dsp[:, 3 * q + 2], mixT, t,
                                    d_filled)

            pe.sem_inc(e_xt, 2)
            pe.wait_ge(d_dve, 4 + 10 * KT)
            pe.wait_ge(e_split, 2 + KT)

            def project(i, b, rows, ev):
                pe.wait_ge(e_evac, i + 1)
                for m in range(2):
                    for k in range(KT):
                        for n, (wp, hp) in enumerate(PASSES):
                            mm = pe.matmul(ps[0:rows, 2 * b + m, :], mT[:, k, hp, ds(i * P, rows)],
                                           wo[:, k, wp, 512 * m:512 * m + 512],
                                           start=(k == 0 and n == 0), stop=(k == KT - 1 and n == 2))
                mm.then_inc(e_filled, 1)

            def transposes2(i, b, rows):
                pe.wait_ge(e_xn, i + 1)
                pe.wait_ge(e_tmp, 2 * i + 1)
                for k in range(KT):
                    mm = pe.transpose(ps[:, 4 + 2 * b + k // 4, (k % 4) * P:(k % 4) * P + rows],
                                      exn[0:rows, b, k * P:(k + 1) * P], ident[0:rows, 0:rows])
                mm.then_inc(e_xt, 1)

            for n in range(5):
                pe.wait_ge(m_loaded[n], 32)
            project(0, 0, P, None)
            with nc.tensor.Fori(0, NT // 2 - 1) as it:
                for b in range(2):
                    project(2 * it + 1 + b, 1 - b, P, None)
                    transposes2(2 * it + b, b, P)
            project(NT - 1, 1, P, None)
            transposes2(NT - 2, 0, P)
            project(NT, 0, TS, None)
            transposes2(NT - 1, 1, P)
            transposes2(NT, 0, TS)

            pe.sem_inc(f_filled, 10)
            pe.wait_ge(e_hT, 2 * (NT + 1))
            with nc.tensor.Fori(0, NF) as f:
                for s in range(2):
                    pe.wait_ge(f_split, 3 * f + s + 4)
                    for n, (t, w) in enumerate(BLOCKS):
                        u = 5 * s + n
                        pe.wait_ge(f_act, 10 * f + (u + 3 if u >= 8 else u + 9 if u < 2 else u + 1))
                        product(ps[:, u % 8, 0:w], w, 0, KT, fsp[:, s], hT, t, f_filled)

            pe.wait_ge(f_act, 10 * NF + 10)
            pe.wait_ge(f_split, 3 * NF + 3)

            def down(i, b, rows, blk, t):
                pe.wait_ge(g_evac, i + 1)
                for m in range(2):
                    for k in range(NF):
                        for n, (wp, hp) in enumerate(PASSES):
                            mm = pe.matmul(ps[0:rows, 2 * b + m, :], hb[blk][:, k, hp, t:t + rows],
                                           wd[:, k, wp, 512 * m:512 * m + 512],
                                           start=(k == 0 and n == 0), stop=(k == NF - 1 and n == 2))
                mm.then_inc(g_filled, 1)

            with nc.tensor.Fori(0, 2) as ib:
                for s in range(2):
                    for q in range(2):
                        pe.wait_ge(hb_loaded[s][q], 32 * ib + 32)
                        for b in range(2):
                            down(8 * ib + 4 * s + 2 * q + b, b, P, s, 256 * q + 128 * b)
            pe.wait_ge(hs_loaded, 32)
            down(NT, 0, TS, 0, 0)


_IN = [("params", (P, NPAR)), ("rel_table", (8, 513)), ("x_prompt", (TP, D)), ("x_sample", (TS, D)),
       ("w_mod", (48, P, KT, P)), ("w_in", (36, P, KT, P)), ("cache_k", (4, P, NJ, P)), ("cache_v", (4, P, NJ, P)),
       ("w_rgate", (2, 8, 64, 64)), ("w_branch", (KT, P, KT, P)), ("w_out", (KT, P, D)), ("w_up", (2 * NF, P, KT, P)),
       ("w_down", (NF, P, D)), ("g_final", (1, D))]
_OUT = [("k_prompt", (NJ, P, PAST)), ("k_sample", (NJ, P, TS)), ("v_prompt", (4, P, NJ, P)),
        ("v_sample", (TS, NJ, P)), ("rnn_hold", (P, 32)), ("y_prompt", (TP, D)), ("y_sample", (TS, D)),
        ("ffn_hold", (P, 176))]


def declare(nc):
    a = {}
    for name, shape in _IN:
        a[name] = nc.dram_tensor(f"in_{name}", shape, F32, kind="ExternalInput").ap()
    for name, shape in _OUT:
        a[name] = nc.dram_tensor(f"out_{name}", shape, F32, kind="ExternalOutput").ap()
    return a


def lay_out(i):
    import numpy as np

    def tiles(w):
        k, m = w.shape
        return np.ascontiguousarray(w.reshape(k // P, P, m // P, P).transpose(2, 1, 0, 3))

    def cols(v):
        v = np.asarray(v)
        v = v.reshape(v.shape[:-1] + (v.shape[-1] // P, P))
        return np.moveaxis(v, (-1, -2), (0, 1)).reshape(P, -1)

    c = np.concatenate([i["c_prompt"], i["c_sample"]])
    par = [cols(c), cols(i["mod_mix_b"][0]), cols(i["mod_ffn_b"][0]), cols(i["norm_mix_g"][0]),
           cols(i["norm_ffn_g"][0]), cols(i["rnn_conv_w"][0]), cols(i["rnn_conv_b"][0]), cols(i["rnn_gate_a_b"][0]),
           cols(i["rnn_gate_x_b"][0]), cols(i["rnn_lambda"][0]), cols(i["state_rnn_h"][0, 0]),
           cols(i["state_rnn_conv"][0, 0]), cols(i["ffn_conv_w"][0]), cols(i["ffn_conv_b"][0]),
           cols(i["state_ffn_conv"][0, 0])]
    return {
        "params": np.ascontiguousarray(np.concatenate(par, axis=1)),
        "rel_table": np.ascontiguousarray(i["rel_bias_table"][0].T[:, ::-1]),
        "x_prompt": np.ascontiguousarray(i["x_prompt"][0]),
        "x_sample": np.ascontiguousarray(i["x_sample"][0]),
        "w_mod": np.concatenate([tiles(i["mod_mix_w"][0]), tiles(i["mod_ffn_w"][0])]),
        "w_in": tiles(i["w_in"][0]),
        "cache_k": np.ascontiguousarray(i["cache_k"].reshape(4, P, NJ, P)),
        "cache_v": np.ascontiguousarray(i["cache_v"].reshape(4, P, NJ, P)),
        "w_rgate": np.stack([i["rnn_gate_a_w"][0], i["rnn_gate_x_w"][0]]),
        "w_branch": tiles(i["w_branch"][0]),
        "w_out": np.ascontiguousarray(i["w_out"][0].reshape(KT, P, D)),
        "w_up": tiles(i["ffn_up_w"][0]),
        "w_down": np.ascontiguousarray(i["ffn_down_w"][0].reshape(NF, P, D)),
        "g_final": i["final_norm_g"][None],
    }


def kernel(**inputs):
    import numpy as np
    import concourse.bacc as bacc
    from concourse.bass_utils import run_bass_kernel_spmd

    nc = bacc.Bacc("TRN2", target_bir_lowering=False, num_devices=1)
    a = declare(nc)
    build(nc, a)
    arrays = {f"in_{k}": v for k, v in lay_out({k: np.asarray(v) for k, v in inputs.items()}).items()}
    got = run_bass_kernel_spmd(nc, [arrays], core_ids=[0]).results[0]
    out = {name: np.asarray(got[f"out_{name}"]) for name, _ in _OUT}
    rnn = out["rnn_hold"].reshape(P, NJ, 8)
    ffn = out["ffn_hold"].reshape(P, 2 * NF, 4)

    def rows(v):
        return v.transpose(2, 1, 0).reshape(1, 1, v.shape[2], -1)

    return (out["y_prompt"].reshape(1, TP, D), out["y_sample"].reshape(1, TS, D),
            out["k_prompt"].transpose(2, 0, 1).reshape(1, 1, PAST, 8, HD),
            out["v_prompt"].reshape(1, 1, PAST, 8, HD),
            out["k_sample"].transpose(2, 0, 1).reshape(1, 1, TS, 8, HD),
            out["v_sample"].reshape(1, 1, TS, 8, HD),
            rows(rnn[:, :, 0:3]), rows(rnn[:, :, 3:6]),
            rows(rnn[:, :, 6:7]).reshape(1, 1, -1), rows(rnn[:, :, 7:8]).reshape(1, 1, -1),
            rows(ffn[:, :, 0:2]), rows(ffn[:, :, 2:4]))
```

```python
from contextlib import ExitStack

import concourse.bass as bass
from concourse import mybir

ALU = mybir.AluOpType
ACT = mybir.ActivationFunctionType
F32 = mybir.dt.float32
F16 = mybir.dt.float16
ds = bass.ds

P = 128
D = 1024
KT = D // P
TP, TS = 2048, 64
T = TP + TS
NT = TP // P
HD = 64
NJ = 4
PAST = 512
KEYS = TP + PAST + TS
BAND = 640
DFF = 2816
NF = DFF // P
EPS = 1e-6
WS, XS = 256.0, 8.0
CS = 1.0 / (WS * XS)
MASKED = 1e30
ARENA = 53200
MLOTS = [(0, 384), (384, 512), (896, 512), (1408, 512), (1920, 192)]
BLOCKS = [(0, 512), (512, 512), (1024, 512), (1536, 512), (2048, 64)]
PASSES = [(0, 0), (0, 1), (1, 0)]

COLS = {}
NPAR = 0
for _name, _n in (("c", 16), ("mod_b", 48), ("g_mix", 8), ("g_ffn", 8), ("cw", 16), ("cb", 4), ("ba", 4),
                  ("bx", 4), ("lam", 4), ("h0", 4), ("cstate", 12), ("fw", 132), ("fb", 44), ("fstate", 88)):
    COLS[_name] = NPAR
    NPAR += _n

WQ, WK, WV, WRX, WRG, WGA, WGB = 0, 4, 8, 12, 16, 20, 28


def build(nc, a):
    ctx = ExitStack()
    with ctx:
        def sem(name):
            return ctx.enter_context(nc.semaphore(name))

        arena = ctx.enter_context(nc.sbuf_tensor("arena", [P, ARENA], F32))
        ps = ctx.enter_context(nc.psum_tensor("ps", [P, 8, 512], F32))

        def carve(at, n, dt=F32):
            w = n if dt == F32 else (n + 1) // 2
            assert at + w <= ARENA, (at, w)
            v = arena[:, at:at + w]
            return (v if dt == F32 else v.bitcast(dt)), at + w

        at = 0
        hT_, at = carve(at, KT * 2 * T, F16)
        hT = hT_.rearrange("p (k s t) -> p k s t", k=KT, s=2)
        par, at = carve(at, NPAR)
        ident, at = carve(at, P)
        mod, at = carve(at, 96)
        modv = mod.rearrange("p (m f s) -> p m f s", m=2, s=2)
        coef, at = carve(at, 2 * 2 * 2 * KT)
        coefv = coef.rearrange("p (m c s k) -> p m c s k", m=2, c=2, s=2)
        sp8, at = carve(at, 4)
        small, at = carve(at, 64)
        rstd, at = carve(at, 24)
        hold_conv, at = carve(at, 4 * 8)
        holdv = hold_conv.rearrange("p (j c) -> p j c", j=4)
        fhold, at = carve(at, 44 * 4)
        fholdv = fhold.rearrange("p (f c) -> p f c", c=4)
        cs, at = carve(at, 16)
        csv = cs.rearrange("p (k s) -> p k s", s=2)
        modraw, at = carve(at, 64)
        BASE = at

        def col(name, i=0, n=1):
            c = COLS[name] + i
            return par[:, c:c + n]

        mw_, _ = carve(0, 16 * D)
        mw = mw_.rearrange("p (f k m) -> p f k m", f=16, k=KT)
        x_all_, at = carve(BASE + 4 * D, (NT + 1) * D)
        x_all = x_all_.rearrange("p (i d) -> p i d", d=D)
        xT = x_all_.rearrange("p (i k t) -> p i k t", k=KT, t=P)
        xn_, at = carve(at, 2 * D)
        xn = xn_.rearrange("p (s d) -> p s d", s=2)
        junk_, at = carve(at, 2 * D)
        junk = junk_.rearrange("p (s d) -> p s d", s=2)
        sgc, at = carve(at, 16)
        arow, at = carve(at, 16 * P)
        tab, at = carve(at, 513)
        tabr, at = carve(at, 768)

        at = BASE
        wst_, at = carve(at, 2 * D)
        wst = wst_.rearrange("p (s k m) -> p s k m", s=2, k=KT)
        wsp_, at = carve(at, 2 * 2 * D, F16)
        wsp = wsp_.rearrange("p (s h k m) -> p s h k m", s=2, h=2, k=KT)
        LB = T + 3
        bufA, at = carve(at, TP + 3 + TS + 3)
        bufX, at = carve(at, LB)
        bufI, at = carve(at, LB)
        bufT, at = carve(at, LB)
        bufG, at = carve(at, LB)
        rstage_, at = carve(at, 2 * LB, F16)
        rstage = rstage_.rearrange("p (s t) -> p s t", s=2)
        bufR, _ = carve(at - LB, LB)
        bias_, at = carve(at, 2 * BAND)
        bias = bias_.rearrange("p (h n) -> p h n", h=2)
        qs_, at = carve(at, 2 * T, F16)
        qs = qs_.rearrange("p (h t) -> p h t", h=2)
        khh_, at = carve(at, 2 * KEYS, F16)
        khh = khh_.rearrange("p (h t) -> p h t", h=2)
        kll_, at = carve(at, 2 * KEYS, F16)
        kll = kll_.rearrange("p (h t) -> p h t", h=2)
        vv_, at = carve(at, 21 * P)
        vv = vv_.rearrange("p (i d) -> p i d", d=P)
        kf, at = carve(at, PAST + TS)
        pr_, at = carve(at, 2 * BAND)
        pr = pr_.rearrange("p (h n) -> p h n", h=2)
        pt_, at = carve(at, 2 * BAND)
        pt = pt_.rearrange("p (h n) -> p h n", h=2)
        osb, at = carve(at, P)
        ost_, at = carve(at, 2 * T, F16)
        ost = ost_.rearrange("p (s t) -> p s t", s=2)
        kc_, at = carve(at, 4 * P)
        kc = kc_.rearrange("p (c d) -> p c d", c=4)
        gw_, at = carve(at, 2 * P)
        gw = gw_.rearrange("p (g m) -> p g m", g=2)
        gbias, at = carve(at, 2)
        mark, at = carve(at, 2)
        least, at = carve(at, 2)
        sm, at = carve(at, 2)
        rs, at = carve(at, 2)

        mixT_, at = carve(BASE, KT * 2 * T, F16)
        mixT = mixT_.rearrange("p (k s t) -> p k s t", k=KT, s=2)
        dst_, at = carve(at, 3 * D)
        dst = dst_.rearrange("p (s k m) -> p s k m", s=3, k=KT)
        dsp_, at = carve(at, 6 * 2 * D, F16)
        dsp = dsp_.rearrange("p (s h k m) -> p s h k m", s=6, h=2, k=KT)
        mstage_, at = carve(at, 2 * T, F16)
        mstage = mstage_.rearrange("p (s t) -> p s t", s=2)
        sig_, at = carve(at, 4 * 512)
        sig = sig_.rearrange("p (b g t) -> p b g t", b=2, g=2)
        mrg_, at = carve(at, 2 * 512)
        mrg = mrg_.rearrange("p (b t) -> p b t", b=2)
        crow_, at = carve(at, 2 * D)
        crow = crow_.rearrange("p (s d) -> p s d", s=2)
        dmw, at = carve(at, D)
        djunk, at = carve(at, D, F16)
        dsum, at = carve(at, 16)

        mT_, at = carve(BASE, KT * 2 * T, F16)
        mT = mT_.rearrange("p (k s t) -> p k s t", k=KT, s=2)
        gate1_, at = carve(at, 2 * D)
        gate1 = gate1_.rearrange("p (s d) -> p s d", s=2)
        at += D
        wo_, at = carve(at, KT * 2 * D, F16)
        wo = wo_.rearrange("p (k h m) -> p k h m", k=KT, h=2)
        ex_, at = carve(at, 2 * D)
        ex = ex_.rearrange("p (b d) -> p b d", b=2)
        exn_, at = carve(at, 2 * D)
        exn = exn_.rearrange("p (b d) -> p b d", b=2)
        etmp_, at = carve(at, 2 * D)
        etmp = etmp_.rearrange("p (s k t) -> p s k t", s=2, k=KT)
        est = [dst[:, i].rearrange("p k m -> p (k m)") for i in range(3)] + [
            exn[:, 0], exn[:, 1], etmp_[:, 0:D], etmp_[:, D:2 * D], ex[:, 0]]

        LF = T + 2
        fsp_, at = carve(BASE, 2 * 2 * D, F16)
        fsp = fsp_.rearrange("p (s h k m) -> p s h k m", s=2, h=2, k=KT)
        ubuf, at = carve(at, LF + 2)
        yval, at = carve(at, LF)
        ygate, at = carve(at, LF)
        hstage_, at = carve(at, 2 * LF, F16)
        hstage = hstage_.rearrange("p (s t) -> p s t", s=2)
        fst_, at = carve(at, 2 * D)
        fst = fst_.rearrange("p (s m) -> p s m", s=2)
        wd_, at = carve(at, NF * 2 * D, F16)
        wd = wd_.rearrange("p (k h m) -> p k h m", k=NF, h=2)

        hb0_, at = carve(0, NF * 2 * 512, F16)
        gate2_, at = carve(at, 2 * D)
        gate2 = gate2_.rearrange("p (s d) -> p s d", s=2)
        gfin, at = carve(at, D)
        gx_, at = carve(at, 2 * D)
        gx = gx_.rearrange("p (b d) -> p b d", b=2)
        assert at <= KT * T
        hb1_, at = carve(BASE, NF * 2 * 512, F16)
        assert at <= BASE + 4 * D + LF + 2 + 3 * LF
        hb = [h.rearrange("p (k s t) -> p k s t", k=NF, s=2) for h in (hb0_, hb1_)]

        bias_d = nc.dram_tensor("bias_rows", (8, 768), F32, kind="Internal").ap()
        band_d = nc.dram_tensor("band", (P, 8, BAND), F32, kind="Internal").ap()
        gate_d = nc.dram_tensor("gate_rows", (4, D), F32, kind="Internal").ap()
        mix_d = nc.dram_tensor("mixer_outputs", (8, P, 2, T), F16, kind="Internal").ap()
        merged_d = nc.dram_tensor("merged", (KT, P, 2, T), F16, kind="Internal").ap()
        x1_d = nc.dram_tensor("x_after_mixers", (T, D), F32, kind="Internal").ap()
        hid_d = nc.dram_tensor("ffn_hidden", (NF, P, 2, T), F16, kind="Internal").ap()

        par_loaded = sem("par_loaded")
        tab_loaded = sem("tab_loaded")
        tab_ready = sem("tab_ready")
        bias_rows_stored = sem("bias_rows_stored")
        band_stored = sem("band_stored")
        x_loaded = [sem(f"x_loaded{i}") for i in range(5)]
        mw_loaded = [sem(f"mw_loaded{i}") for i in range(4)]
        arow_act = sem("arow_act")
        arow_dve = sem("arow_dve")
        arow_filled = sem("arow_filled")
        ident_ready = sem("ident_ready")
        silu_sig = sem("silu_sig")
        silu_ready = sem("silu_ready")
        mod_filled = sem("mod_filled")
        dve_seq = sem("dve_seq")
        ss_ready = sem("ss_ready")
        var_ready = sem("var_ready")
        std_ready = sem("std_ready")
        rstd_ready = sem("rstd_ready")
        xn_ready = sem("xn_ready")
        xT_filled = sem("xT_filled")
        xT_act = sem("xT_act")
        xT_dve = sem("xT_dve")
        modulated = sem("modulated")
        hi_ready = sem("hi_ready")
        hT_ready = sem("hT_ready")
        gate_rows_stored = sem("gate_rows_stored")
        sp_a = sem("sp_a")
        sp_v = sem("sp_v")

        st_loaded = [sem(f"st_loaded{i}") for i in range(2)]
        w_hi = sem("w_hi")
        w_split = sem("w_split")
        gw_zero = sem("gw_zero")
        gw_loaded = sem("gw_loaded")
        aux_loaded = sem("aux_loaded")
        kc_loaded = sem("kc_loaded")
        v_loaded = sem("v_loaded")
        gap_ready = sem("gap_ready")
        c_filled = sem("c_filled")
        c_act = sem("c_act")
        c_dve = sem("c_dve")
        c_hi = sem("c_hi")
        kdup = sem("kdup")
        xc_ready = sem("xc_ready")
        rg_act = sem("rg_act")
        rg_dve = sem("rg_dve")
        kf_ready = sem("kf_ready")
        kf_stored = sem("kf_stored")
        v_stored = sem("v_stored")
        rnn_stored = sem("rnn_stored")
        attn_stored = sem("attn_stored")
        held = sem("held")
        hold_stored = sem("hold_stored")
        s_filled = sem("s_filled")
        s_added = sem("s_added")
        p_ready = sem("p_ready")
        r_ready = sem("r_ready")
        t_filled = sem("t_filled")
        t_act = sem("t_act")
        t_dve = sem("t_dve")
        o_filled = sem("o_filled")
        o_ready = sem("o_ready")
        ot_filled = sem("ot_filled")
        ot_hi = sem("ot_hi")
        ot_ready = sem("ot_ready")
        bias_masked = sem("bias_masked")

        d_loaded = [sem(f"d_loaded{i}") for i in range(3)]
        mix_loaded = sem("mix_loaded")
        d_hi = sem("d_hi")
        d_split = sem("d_split")
        d_filled = sem("d_filled")
        d_act = sem("d_act")
        d_dve = sem("d_dve")
        d_step = sem("d_step")
        d_mhi = sem("d_mhi")
        d_mlo = sem("d_mlo")
        m_stored = sem("m_stored")
        crow_loaded = sem("crow_loaded")
        crow_sig = sem("crow_sig")
        crow_ready = sem("crow_ready")
        dmw_loaded = sem("dmw_loaded")
        dm_step = sem("dm_step")
        dm_used = sem("dm_used")
        dm_kept = sem("dm_kept")
        gate_ready = sem("gate_ready")

        e_loaded = [sem(f"e_loaded{i}") for i in range(2)]
        e_whi = sem("e_whi")
        e_split = sem("e_split")
        m_loaded = [sem(f"m_loaded{i}") for i in range(5)]
        gate1_loaded = sem("gate1_loaded")
        ex_loaded = [sem(f"ex_loaded{i}") for i in range(2)]
        x1_stored = [sem(f"x1_stored{i}") for i in range(2)]
        e_filled = sem("e_filled")
        e_gated = sem("e_gated")
        e_evac = sem("e_evac")
        e_ss = sem("e_ss")
        e_var = sem("e_var")
        e_std = sem("e_std")
        e_rstd = sem("e_rstd")
        e_xn = sem("e_xn")
        e_xt = sem("e_xt")
        e_tmp = sem("e_tmp")
        e_hi = sem("e_hi")
        e_hT = sem("e_hT")

        f_loaded = [sem(f"f_loaded{i}") for i in range(2)]
        f_hi = sem("f_hi")
        f_split = sem("f_split")
        f_filled = sem("f_filled")
        f_pad = sem("f_pad")
        f_act = sem("f_act")
        f_conv = sem("f_conv")
        f_gelu = sem("f_gelu")
        f_prod = sem("f_prod")
        f_phi = sem("f_phi")
        f_plo = sem("f_plo")
        h_stored = sem("h_stored")

        hb_loaded = [[sem(f"hb_loaded{s}{q}") for q in range(2)] for s in range(2)]
        hb_last = [sem(f"hb_last{q}") for q in range(2)]
        hs_loaded = sem("hs_loaded")
        rows_loaded = sem("rows_loaded")
        gx_loaded = [sem(f"gx_loaded{i}") for i in range(2)]
        g_filled = sem("g_filled")
        g_gated = sem("g_gated")
        g_evac = sem("g_evac")
        g_ss = sem("g_ss")
        g_var = sem("g_var")
        g_std = sem("g_std")
        g_rstd = sem("g_rstd")
        g_y = sem("g_y")
        y_stored = [sem(f"y_stored{i}") for i in range(2)]

        block = ctx.enter_context(nc.Block())

        UNITS = [(WRX, 0), (WRG, 1), (WQ, 0), (WK, 1), (WV, 0)]
        USES = (["A"] * 5 + ["A"] * 5 + ["V"] * 5 + ["A"] * 10 + ["V"] * 5 + ["V"] + ["V"] * 5)
        NU = len(USES)
        NA, NV = USES.count("A"), USES.count("V")
        U_RX, U_RG, U_Q, U_G, U_K, U_KC, U_V = 0, 5, 10, 15, 25, 30, 31

        def drained_before(u):
            e = USES[u]
            return e, USES[:u + 1].count(e)

        def short(p):
            n = P * (p + 1)
            return 0, n, BAND - n

        NUNIT = 2 * (NT + 1)

        @block.sync
        def _(sp):
            sp.dma_start(par, a["params"]).then_inc(par_loaded, 16)
            sp.dma_start(tab[0:8, :], a["rel_table"]).then_inc(tab_loaded, 16)
            xp = a["x_prompt"].rearrange("(g i p) d -> g p i d", p=P, i=4)
            for g in range(4):
                sp.dma_start(x_all[:, 4 * g:4 * g + 4, :], xp[g]).then_inc(x_loaded[g], 16)
            sp.dma_start(x_all[0:TS, NT, :], a["x_sample"]).then_inc(x_loaded[4], 16)
            for g in range(4):
                sp.dma_start(mw[:, 4 * g:4 * g + 4].rearrange("p f k m -> p f (k m)"),
                             a["w_mod"][4 * g:4 * g + 4].rearrange("f p k m -> p f (k m)")).then_inc(mw_loaded[g], 16)

            for w, s in UNITS[0:2]:
                sp.dma_start(wst[:, s], a["w_in"][w]).then_inc(st_loaded[s], 16)
            with nc.sync.Fori(0, NJ) as j:
                for i, (w, s) in enumerate(UNITS[2:5] + [(w + 1, s) for w, s in UNITS[0:2]]):
                    sp.wait_ge(w_split, 5 * j + (6, 7, 8, 10, 9)[i])
                    sp.dma_start(wst[:, s], a["w_in"][ds(j + w, 1)].rearrange("a p k m -> p (a k) m"))\
                        .then_inc(st_loaded[s], 16)
                    if i == 0:
                        sp.wait_ge(gw_zero, 1)
                        sp.wait_ge(band_stored, 16)
                        sp.wait_ge(c_filled, NU * j + NU)
                        for b in range(2):
                            sp.dma_start(gw[64 * b:64 * b + 64, :, 64 * b:64 * b + 64],
                                         a["w_rgate"][:, ds(2 * j + b, 1)].rearrange("g n i m -> i (g n) m"))\
                                .then_inc(gw_loaded, 16)
                        sp.wait_ge(ot_ready, (NT + 1) * (j + 1))
                        sp.wait_ge(v_stored, 32 * j + 32)
                        sp.dma_start(kc, a["cache_k"][:, :, ds(j, 1), :].rearrange("c p j d -> p (c j) d"))\
                            .then_inc(kc_loaded, 16)
                        sp.dma_start(vv[:, NT:NT + 4, :],
                                     a["cache_v"][:, :, ds(j, 1), :].rearrange("c p j d -> p (c j) d"))\
                            .then_inc(v_loaded, 16)
                        sp.dma_start(bias, band_d[:, ds(2 * j, 2), :]).then_inc(aux_loaded, 16)

            sp.wait_ge(ot_ready, (NT + 1) * (NJ + 1))
            sp.wait_ge(kf_stored, 32 * (NJ + 1))
            sp.wait_ge(v_stored, 32 * (NJ + 1))
            sp.wait_ge(rnn_stored, 32 * (NJ + 1))

            def merge_tiles(it, q):
                for i, src in enumerate((a["w_in"][ds(2 * it + q + WGA, 1)], a["w_in"][ds(2 * it + q + WGB, 1)],
                                         a["w_branch"][ds(2 * it + q, 1)])):
                    sp.wait_ge(d_split, 6 * it + 3 * q + i + 1)
                    sp.dma_start(dst[:, i], src.rearrange("a p k m -> p (a k) m")).then_inc(d_loaded[i], 16)

            def later_tile(n):
                sp.wait_ge(dm_used, n + 1)
                sp.dma_start(dmw, a["w_mod_rest"][ds(n, 1)].rearrange("a p k -> (a p) k")).then_inc(dmw_loaded, 16)

            merge_tiles(0, 0)
            sp.wait_ge(attn_stored, 16 * (NJ + 1))
            for s in range(2):
                sp.dma_start(crow[:, s, :], a["c"][s:s + 1, :].to_broadcast([P, D])).then_inc(crow_loaded, 16)
            for k in range(KT):
                sp.dma_start(mixT[:, k], mix_d[k]).then_inc(mix_loaded, 16)
            merge_tiles(0, 1)
            for n in range(4):
                later_tile(n)
            with nc.sync.Fori(1, KT // 2) as it:
                merge_tiles(it, 0)
                for n in range(4):
                    later_tile(8 * it - 4 + n)
                merge_tiles(it, 1)
                for n in range(4):
                    later_tile(8 * it + n)
            sp.wait_ge(gate_ready, 1)
            for s in range(2):
                sp.dma_start(gate_d[s:s + 1, :].rearrange("g (k p) -> p (g k)", p=P), modv[:, 0, 16:24, s],
                             allow_slow_non_contiguous=True)\
                    .then_inc(gate_rows_stored, 16)
            for n in range(28, 32):
                later_tile(n)

            def out_tile(k):
                sp.dma_start(est[k], a["w_out"][k]).then_inc(e_loaded[k > 2], 16)

            sp.wait_ge(d_split, 3 + 3 * KT)
            for k in range(3):
                out_tile(k)

            sp.wait_ge(d_filled, 40 + 20 * KT)
            sp.wait_ge(m_stored, 16 * (KT + 1))
            sp.wait_ge(d_step, 5 * KT)
            sp.wait_ge(dm_kept, 1 + KT // 2)
            for k in range(3, KT):
                out_tile(k)
            for n, (t, w) in enumerate(MLOTS):
                for part in range(2):
                    sp.dma_start(mT[:, :, part, t:t + w], merged_d[:, :, part, t:t + w].rearrange("k p t -> p k t"))\
                        .then_inc(m_loaded[n], 16)
                if n == 0:
                    sp.wait_ge(gate_rows_stored, 32)
                    sp.wait_ge(e_split, 3)
                    for s in range(2):
                        sp.dma_start(gate1[:, s, :], gate_d[s:s + 1, :].to_broadcast([P, D])).then_inc(gate1_loaded, 16)
                    sp.wait_ge(e_split, KT)
                    for b in range(2):
                        sp.dma_start(ex[:, b], a["x_prompt"][b * P:(b + 1) * P, :]).then_inc(ex_loaded[b], 16)
            with nc.sync.Fori(1, NT // 2) as it:
                for b in range(2):
                    sp.wait_ge(x1_stored[b], 16 * it + 16)
                    sp.wait_ge(e_xn, 2 * it + b - 1)
                    sp.dma_start(ex[:, b], a["x_prompt"][ds(2 * P * it + b * P, P), :]).then_inc(ex_loaded[b], 16)
            sp.wait_ge(x1_stored[0], 16 * (NT // 2) + 16)
            sp.wait_ge(e_xn, NT - 1)
            sp.dma_start(ex[0:TS, 0], a["x_sample"]).then_inc(ex_loaded[0], 16)

            sp.wait_ge(gate_ready, 2)
            for s in range(2):
                sp.dma_start(gate_d[2 + s:3 + s, :].rearrange("g (k p) -> p (g k)", p=P), modv[:, 1, 16:24, s],
                             allow_slow_non_contiguous=True)\
                    .then_inc(gate_rows_stored, 16)

            def ffn_tile(src, s):
                sp.dma_start(fst[:, s], src).then_inc(f_loaded[s], 16)

            sp.wait_ge(e_filled, NT + 1)
            ffn_tile(a["w_up"][0].rearrange("p k m -> p (k m)"), 0)

            def ffn_tiles(f, last):
                sp.wait_ge(f_split, 3 * f + 2)
                ffn_tile(a["w_up"][ds(f + NF, 1)].rearrange("a p k m -> p (a k m)"), 1)
                sp.wait_ge(f_split, 3 * f + 4)
                ffn_tile(a["w_down"][ds(f, 1)].rearrange("a p m -> p (a m)"), 0)
                if not last:
                    sp.wait_ge(f_split, 3 * f + 6)
                    ffn_tile(a["w_up"][ds(f + 1, 1)].rearrange("a p k m -> p (a k m)"), 0)

            with nc.sync.Fori(0, NF - 1) as f:
                ffn_tiles(f, False)
            ffn_tiles(NF - 1, True)

            sp.wait_ge(f_filled, 10 * NF + 10)
            sp.wait_ge(x1_stored[0], 16 * (NT // 2 + 2))
            sp.wait_ge(x1_stored[1], 16 * (NT // 2 + 1))

            def hidden(ib, s):
                for q in range(2):
                    for part in range(2):
                        sp.dma_start(hb[s][:, :, part, 256 * q:256 * q + 256],
                                     hid_d[:, :, part, 1024 * ib + 512 * s + 256 * q:
                                           1024 * ib + 512 * s + 256 * q + 256].rearrange("k p t -> p k t"))\
                            .then_inc(hb_loaded[s][q], 16)

            def first_hidden(k0, k1, sems):
                for q in range(2):
                    for part in range(2):
                        sp.dma_start(hb[0][:, k0:k1, part, 256 * q:256 * q + 256],
                                     hid_d[k0:k1, :, part, 256 * q:256 * q + 256].rearrange("k p t -> p k t"))\
                            .then_inc(sems[q], 16)

            def residual(row, b, rows=P):
                sp.dma_start(gx[0:rows, b], x1_d[ds(row, rows), :]).then_inc(gx_loaded[b], 16)

            sp.wait_ge(h_stored, 32 * NF)
            first_hidden(0, NF - 1, hb_loaded[0])
            sp.wait_ge(gate_rows_stored, 64)
            for s in range(2):
                sp.dma_start(gate2[:, s, :], gate_d[2 + s:3 + s, :].to_broadcast([P, D])).then_inc(rows_loaded, 16)
            sp.dma_start(gfin, a["g_final"].to_broadcast([P, D])).then_inc(rows_loaded, 16)
            residual(0, 0)
            residual(P, 1)
            sp.wait_ge(h_stored, 32 * NF + 32)
            first_hidden(NF - 1, NF, hb_last)
            sp.wait_ge(f_split, 3 * NF + 3)
            hidden(0, 1)

            def residuals(i, n):
                for b in range(2):
                    sp.wait_ge(y_stored[b], n)
                    residual(i * P + b * P, b)

            residuals(2, 32)
            residuals(4, 48)
            sp.wait_ge(g_filled, 4)
            hidden(1, 0)
            residuals(6, 64)
            residuals(8, 80)
            sp.wait_ge(g_filled, 8)
            hidden(1, 1)
            residuals(10, 96)
            residuals(12, 112)
            sp.wait_ge(g_filled, 12)
            for part in range(2):
                sp.dma_start(hb[0][:, :, part, 0:TS], hid_d[:, :, part, TP:T].rearrange("k p t -> p k t"))\
                    .then_inc(hs_loaded, 16)
            residuals(14, 128)
            sp.wait_ge(y_stored[0], 16 * (NT // 2 + 1))
            residual(TP, 0, TS)

        @block.gpsimd
        def _(pool):
            pool.memset(ident, 0.0).then_inc(ident_ready, 1)
            pool.wait_ge(ident_ready, 1)
            pool.affine_select(out=ident, in_=ident, compare_op=ALU.not_equal, fill=1.0, base=0,
                               pattern=[[-1, P]], channel_multiplier=1).then_inc(ident_ready, 1)
            pool.wait_ge(tab_ready, 2)
            pool.dma_start(bias_d[:, 0:767], tabr[0:8, 0:767]).then_inc(bias_rows_stored, 16)
            pool.wait_ge(bias_rows_stored, 16)
            pool.dma_start(band_d.rearrange("q h n -> h q n"),
                           bass.AP(bias_d.tensor, P - 1, [[768, 8], [-1, P], [1, BAND]]))\
                .then_inc(band_stored, 16)
            pool.wait_ge(hT_ready, NT + 1)
            pool.memset(gw, 0.0).then_inc(gw_zero, 1)
            pool.memset(bufI[:, TP:TP + 3], 0.0).then_inc(gap_ready, 1)
            pool.memset(bufG[:, TP:TP + 3], 0.0).then_inc(gap_ready, 1)

        @block.scalar
        def _(act):
            act.sem_inc(c_act, NA)
            act.wait_ge(par_loaded, 16)
            act.activation(sgc, col("c", 0, 16), ACT.Sigmoid).then_inc(silu_sig, 1)
            act.activation(small[:, 0:4], col("lam", 0, 4), ACT.Abs).then_inc(sp_a, 1)
            act.wait_ge(sp_a, 1)
            act.activation(small[:, 4:8], small[:, 0:4], ACT.Exp, scale=-1.0).then_inc(sp_a, 1)
            for g in range(5):
                tiles = range(4 * g, min(4 * g + 4, NT + 1))
                rows = P if g < 4 else TS
                act.wait_ge(x_loaded[g], 16)
                for i in tiles:
                    if i >= 2:
                        act.wait_ge(ss_ready, i - 1)
                    act.activation(junk[0:rows, i % 2], x_all[0:rows, i, :], ACT.Square,
                                   accum_out=rstd[0:rows, i:i + 1]).then_inc(ss_ready, 1)
                act.wait_ge(var_ready, g + 1)
                act.activation(rstd[0:rows, tiles[0]:tiles[-1] + 1], rstd[0:rows, tiles[0]:tiles[-1] + 1],
                               ACT.Sqrt).then_inc(std_ready, 1)
                for i in tiles:
                    act.wait_ge(xT_filled, i + 1)
                    act.activation(xT[:, i, 4:8, 0:rows],
                                   ps[:, 2 * (i % 2) + 1, :].rearrange("p (k t) -> p k t", t=P)[:, :, 0:rows],
                                   ACT.Copy).then_inc(xT_act, 1)
            for g in range(2):
                act.wait_ge(arow_filled, g + 1)
                act.activation(arow[0:2, 512 * g:512 * g + 512], ps[0:2, 4 + g, :], ACT.Copy).then_inc(arow_act, 1)
            def split_hi(i, s, loads, free):
                act.wait_ge(st_loaded[s], 16 * loads)
                if free is not None:
                    act.wait_ge(c_filled, free)
                act.activation(wsp[:, s, 0], wst[:, s], ACT.Copy, scale=WS).then_inc(w_hi, 1)

            split_hi(0, 0, 1, None)
            split_hi(1, 1, 1, None)
            for n in range(5):
                act.wait_ge(modulated, n + 1)
                for i in range(4 * n, min(4 * n + 4, NT + 1)):
                    rows = P if i < NT else TS
                    act.activation(hT[:, :, 0, i * P:i * P + rows], xT[:, i, :, 0:rows], ACT.Copy)\
                        .then_inc(hi_ready, 1)

            act.sem_inc(kf_stored, 32)
            act.sem_inc(v_stored, 32)
            act.sem_inc(rnn_stored, 32)
            act.sem_inc(attn_stored, 16)
            act.wait_ge(band_stored, 16)

            with nc.scalar.Fori(0, NJ) as j:
                def filled(u):
                    act.wait_ge(c_filled, NU * j + NU + u + 1)
                    return ps[:, u % 8, :]

                for n, (t, w) in enumerate(BLOCKS):
                    o = 3 if t < TP else 6
                    act.activation(bufA[:, t + o:t + o + w], filled(U_RX + n)[:, 0:w], ACT.Copy, scale=CS)\
                        .then_inc(c_act, 1)
                act.activation(bufA[:, 0:3], ident[:, 0:3], ACT.Copy, scale=0.0).then_inc(rg_act, 1)
                act.activation(bufA[:, TP + 3:TP + 6].rearrange("p (a b) -> p a b", a=1),
                               col("cstate", 0, 12).rearrange("p (j b) -> p j b", b=3)[:, ds(j, 1), :],
                               ACT.Copy).then_inc(rg_act, 1)
                split_hi(2, 0, 3 * j + 2, NU * j + NU + 5)
                for n, (t, w) in enumerate(BLOCKS):
                    o = 0 if t < TP else 3
                    act.activation(bufG[:, t + o:t + o + w], filled(U_RG + n)[:, 0:w], ACT.Gelu_apprx_tanh,
                                   scale=CS).then_inc(c_act, 1)
                split_hi(3, 1, 2 * j + 2, NU * j + NU + 10)
                for n, (t, w) in enumerate(BLOCKS):
                    src = filled(U_Q + n)
                    act.activation(qs[0:64, 0, t:t + w], src[0:64, 0:w], ACT.Copy, scale=-CS * HD ** -0.5)
                    act.activation(qs[64:128, 1, t:t + w], src[64:128, 0:w], ACT.Copy, scale=-CS * HD ** -0.5)\
                        .then_inc(c_hi, 1)
                split_hi(4, 0, 3 * j + 3, NU * j + NU + 15)
                for n, (t, w) in enumerate(BLOCKS):
                    o = 0 if t < TP else 3
                    for g, gate in enumerate((bufA, bufI)):
                        act.activation(gate[:, t + o:t + o + w], filled(U_G + 2 * n + g)[:, 0:w], ACT.Sigmoid,
                                       bias=gbias[:, g:g + 1]).then_inc(c_act, 1)

                def k_hi(n):
                    if n < 5:
                        t, w = BLOCKS[n]
                        kt, u, sc = (t if t < TP else TP + PAST), U_K + n, CS
                    else:
                        kt, w, u, sc = TP, PAST, U_KC, 1.0
                    src = filled(u)
                    if n == 3:
                        act.wait_ge(kf_stored, 32 * j + 32)
                    if n == 3 or n == 4:
                        o = 0 if n == 3 else PAST
                        act.activation(kf[:, o:o + w], src[:, 0:w], ACT.Copy, scale=CS).then_inc(kf_ready, 1)
                    for h in range(2):
                        own = slice(64 * h, 64 * h + 64)
                        k = act.activation(khh[own, h, kt:kt + w], src[own, 0:w], ACT.Copy, scale=sc)
                    k.then_inc(c_hi, 1)

                k_hi(0)
                k_hi(1)
                act.wait_ge(rg_dve, 10 * j + 2)
                act.activation(bufT[:, 0:LB], bufA[:, 0:LB], ACT.Tanh).then_inc(rg_act, 1)
                act.activation(bufA[:, 0:LB], bufA[:, 0:LB], ACT.Exp, scale=-1.0).then_inc(rg_act, 1)
                k_hi(2)
                k_hi(3)
                act.wait_ge(rg_dve, 10 * j + 5)
                act.activation(bufT[:, 0:LB], bufT[:, 0:LB], ACT.Sqrt).then_inc(rg_act, 1)
                k_hi(4)
                k_hi(5)
                act.wait_ge(rg_dve, 10 * j + 9)
                act.wait_ge(rnn_stored, 32 * j + 32)
                act.activation(rstage[:, 0, :], bufX, ACT.Copy, scale=XS).then_inc(rg_act, 1)

                act.dma_start(a["k_prompt"][ds(j, 1)].rearrange("j p t -> (j p) t"), kf[:, 0:PAST])\
                    .then_inc(kf_stored, 16)
                act.dma_start(a["k_sample"][ds(j, 1)].rearrange("j p t -> (j p) t"), kf[:, PAST:PAST + TS])\
                    .then_inc(kf_stored, 16)
                act.wait_ge(rg_dve, 10 * j + 10)
                act.dma_start(mix_d[ds(j + NJ, 1), :, :, 0:TP].rearrange("j p s t -> (j p) s t"),
                              rstage[:, :, 0:TP]).then_inc(rnn_stored, 16)
                act.dma_start(mix_d[ds(j + NJ, 1), :, :, TP:T].rearrange("j p s t -> (j p) s t"),
                              rstage[:, :, TP + 3:LB]).then_inc(rnn_stored, 16)
                act.wait_ge(c_dve, NV * j + 2 * NV)
                act.dma_start(a["v_prompt"][:, :, ds(j, 1), :].rearrange("c p j d -> p (c j) d"),
                              vv[:, NT - 4:NT, :]).then_inc(v_stored, 16)
                act.dma_start(a["v_sample"][:, ds(j, 1), :].rearrange("p j d -> p (j d)"),
                              vv[0:TS, NT + 4, :]).then_inc(v_stored, 16)

                def exps(n, h, rows, w):
                    act.wait_ge(s_added, n)
                    act.activation(pr[0:rows, h, 0:w], pr[0:rows, h, 0:w], ACT.Exp, scale=-1.0,
                                   bias=least[0:rows, h:h + 1], accum_out=sm[0:rows, h:h + 1]).then_inc(p_ready, 1)

                def probs(n, h, rows, w):
                    act.wait_ge(t_filled, n)
                    m = min(4, (w + P - 1) // P)
                    act.activation(pt[:, h, 0:m * P], ps[:, 4, 0:m * P], ACT.Copy).then_inc(t_act, 1)

                def out_hi(n, t, w):
                    act.wait_ge(ot_filled, n)
                    act.activation(ost[:, 0, ds(t, w)], ps[:, 7, 0:w], ACT.Copy, scale=XS).then_inc(ot_hi, 1)

                un = NUNIT * j
                tn = (NT + 1) * j
                act.wait_ge(attn_stored, 16 * j + 16)
                for p in range(5):
                    if p == 3:
                        split_hi(0, 0, 3 * j + 4, NU * j + 2 * NU)
                        split_hi(1, 1, 2 * j + 3, NU * j + 30 + NU)
                    w = min(BAND, P * (p + 1))
                    pw = min(BAND, P * p)
                    for h in range(2):
                        exps(un + 2 * p + h + 1, h, P, w)
                        if p or h:
                            probs(un + 2 * p + h, 1 - h, P, w if h else pw)
                        if h == 0 and p >= 2:
                            out_hi(tn + p - 1, (p - 2) * P, P)
                with nc.scalar.Fori(5, NT) as p:
                    for h in range(2):
                        exps(un + 2 * p + h + 1, h, P, BAND)
                        probs(un + 2 * p + h, 1 - h, P, BAND)
                        if h == 0:
                            out_hi(tn + p - 1, (p - 2) * P, P)
                exps(un + 2 * NT + 1, 0, TS, PAST + TS)
                probs(un + 2 * NT, 1, P, BAND)
                out_hi(tn + NT - 1, (NT - 2) * P, P)
                exps(un + 2 * NT + 2, 1, TS, PAST + TS)
                probs(un + 2 * NT + 1, 0, TS, PAST + TS)
                probs(un + 2 * NT + 2, 1, TS, PAST + TS)
                out_hi(tn + NT, (NT - 1) * P, P)
                out_hi(tn + NT + 1, TP, TS)
                act.wait_ge(ot_ready, (NT + 1) * (j + 2))
                act.dma_start(mix_d[ds(j, 1)].rearrange("j p s t -> (j p) s t"), ost).then_inc(attn_stored, 16)
            act.dma_start(a["rnn_hold"], hold_conv).then_inc(hold_stored, 16)

            act.sem_inc(d_act, 4)
            act.sem_inc(m_stored, 16)

            def merge_hi(it, q):
                f = 2 * it + q
                for i in range(3):
                    act.wait_ge(d_loaded[i], 16 * f + 16)
                    if i == 0:
                        act.wait_ge(d_filled, 20 * f + 20)
                    act.activation(dsp[:, 3 * q + i, 0], dst[:, i], ACT.Copy, scale=WS).then_inc(d_hi, 1)

            def out_hi_part(k):
                act.wait_ge(e_loaded[k > 2], 48 if k < 3 else 80)
                act.activation(wo[:, k, 0, :], est[k], ACT.Copy, scale=WS).then_inc(e_whi, 1)

            def merge_body(it, last):
                for q in range(2):
                    f = 2 * it + q
                    for n, (t, w) in enumerate(BLOCKS):
                        g, b = 5 * f + n, (5 * q + n) % 2
                        for m in range(2):
                            act.wait_ge(d_filled, 40 + 4 * g + m + 1)
                            act.activation(sig[:, b, m, 0:w], ps[:, 4 * b + m, 0:w], ACT.Sigmoid, scale=CS)\
                                .then_inc(d_act, 1)
                        if n == 0:
                            act.wait_ge(m_stored, 16 * f + 16)
                        act.wait_ge(d_step, g + 1)
                        act.activation(mstage[:, 0, t:t + w], mrg[:, b, 0:w], ACT.Copy).then_inc(d_mhi, 1)
                        if n == 1 and not (last and q == 1):
                            merge_hi(it + q, 1 - q)
                        if last and q == 1 and n == 4:
                            for k in range(3):
                                out_hi_part(k)
                    act.wait_ge(d_mlo, 5 * f + 5)
                    act.dma_start(merged_d[ds(f, 1)].rearrange("f p s t -> (f p) s t"), mstage)\
                        .then_inc(m_stored, 16)

            merge_hi(0, 0)
            act.wait_ge(crow_loaded, 32)
            act.activation(sig_, crow_, ACT.Sigmoid).then_inc(crow_sig, 1)
            act.wait_ge(crow_ready, 1)
            with nc.scalar.Fori(0, KT // 2 - 1) as it:
                merge_body(it, False)
            merge_body(KT // 2 - 1, True)

            for b in range(2):
                act.sem_inc(x1_stored[b], 16)
            for k in range(3, KT):
                out_hi_part(k)

            def square(i, b, rows):
                act.wait_ge(e_evac, i + 3)
                act.dma_start(x1_d[ds(i * P, rows), :], ex[0:rows, b]).then_inc(x1_stored[b], 16)
                act.wait_ge(e_xt, i + 1)
                act.activation(exn[0:rows, b], ex[0:rows, b], ACT.Square, accum_out=rstd[0:rows, b:b + 1])\
                    .then_inc(e_ss, 1)

            def high(i, b, rows):
                for q in range(2):
                    act.wait_ge(e_tmp, 2 * i + q + 4)
                    act.activation(hT[:, 4 * q:4 * q + 4, 0, ds(i * P, rows)],
                                   etmp[:, b, 4 * q:4 * q + 4, 0:rows], ACT.Copy).then_inc(e_hi, 1)

            def scale_rows(i, b, rows):
                act.wait_ge(e_var, i + 1)
                act.activation(rstd[0:rows, 2 + b:3 + b], rstd[0:rows, b:b + 1], ACT.Sqrt).then_inc(e_std, 1)
                act.wait_ge(e_rstd, i + 1)
                act.mul(exn[0:rows, b], ex[0:rows, b], rstd[0:rows, 4 + b:5 + b]).then_inc(e_xn, 1)

            act.wait_ge(e_split, KT)
            square(0, 0, P)
            scale_rows(0, 0, P)
            with nc.scalar.Fori(0, NT // 2 - 1) as it:
                for b in range(2):
                    i = 2 * it + 1 + b
                    square(i, 1 - b, P)
                    high(2 * it + b, b, P)
                    scale_rows(i, 1 - b, P)
            square(NT - 1, 1, P)
            high(NT - 2, 0, P)
            scale_rows(NT - 1, 1, P)
            square(NT, 0, TS)
            high(NT - 1, 1, P)
            scale_rows(NT, 0, TS)
            high(NT, 0, TS)

            act.sem_inc(f_act, 10)
            act.sem_inc(h_stored, 32)
            act.wait_ge(e_xt, NT + 3)

            def up_hi(n, s, count, free):
                act.wait_ge(f_loaded[s], 16 * count)
                if free is not None:
                    act.wait_ge(f_filled, free)
                act.activation(fsp[:, s, 0].rearrange("p k m -> p (k m)"), fst[:, s], ACT.Copy, scale=WS)\
                    .then_inc(f_hi, 1)

            def evacuate(f, s):
                act.wait_ge(f_conv, 6 * f + 3 * s + 1)
                state = col("fstate", 0, 88).rearrange("p (f c) -> p f c", c=2)[:, ds(f + NF * s, 1), :]
                act.activation(ubuf[:, TP + 2:TP + 4].rearrange("p (a c) -> p a c", a=1), state, ACT.Copy)\
                    .then_inc(f_pad, 1)
                for n, (t, w) in enumerate(BLOCKS):
                    o = 2 if t < TP else 4
                    act.wait_ge(f_filled, 10 * f + 10 + 5 * s + n + 1)
                    act.activation(ubuf[:, t + o:t + o + w], ps[:, (5 * s + n) % 8, 0:w], ACT.Copy, scale=CS)\
                        .then_inc(f_act, 1)

            def ffn_body(f, last):
                up_hi(f, 1, f + 1, 10 * f + 10)
                evacuate(f, 0)
                act.wait_ge(f_loaded[0], 16 * (2 * f + 2))
                act.activation(wd[:, ds(f, 1), 0, :].rearrange("p k m -> p (k m)"), fst[:, 0], ACT.Copy, scale=WS)\
                    .then_inc(f_hi, 1)
                if not last:
                    up_hi(f, 0, 2 * f + 3, 10 * f + 15)
                evacuate(f, 1)
                act.wait_ge(f_conv, 6 * f + 7)
                act.activation(ygate, ygate, ACT.Gelu_apprx_tanh).then_inc(f_gelu, 1)
                act.wait_ge(f_prod, f + 1)
                act.wait_ge(h_stored, 32 * f + 32)
                act.activation(hstage[:, 0, :], yval, ACT.Copy).then_inc(f_phi, 1)
                act.wait_ge(f_plo, f + 2)
                act.dma_start(hid_d[ds(f, 1), :, :, 0:TP].rearrange("f p s t -> (f p) s t"), hstage[:, :, 0:TP])\
                    .then_inc(h_stored, 16)
                act.dma_start(hid_d[ds(f, 1), :, :, TP:T].rearrange("f p s t -> (f p) s t"),
                              hstage[:, :, TP + 2:LF]).then_inc(h_stored, 16)

            up_hi(0, 0, 1, None)
            act.activation(ubuf[:, 0:2], ident[:, 0:2], ACT.Copy, scale=0.0).then_inc(f_pad, 1)
            with nc.scalar.Fori(0, NF - 1) as f:
                ffn_body(f, False)
            ffn_body(NF - 1, True)
            act.dma_start(a["ffn_hold"], fhold).then_inc(hold_stored, 16)

            for b in range(2):
                act.sem_inc(y_stored[b], 16)

            def finish(i, b, rows, out):
                act.wait_ge(g_evac, i + 3)
                act.activation(ps[0:rows, 4 + 2 * b:6 + 2 * b, :].rearrange("p b n -> p (b n)"), gx[0:rows, b],
                               ACT.Square, accum_out=rstd[0:rows, b:b + 1]).then_inc(g_ss, 1)
                act.wait_ge(g_var, i + 1)
                act.activation(rstd[0:rows, 2 + b:3 + b], rstd[0:rows, b:b + 1], ACT.Sqrt).then_inc(g_std, 1)
                act.wait_ge(g_y, i + 1)
                act.dma_start(out, gx[0:rows, b]).then_inc(y_stored[b], 16)

            with nc.scalar.Fori(0, NT // 2) as it:
                for b in range(2):
                    finish(2 * it + b, b, P, a["y_prompt"][ds(2 * P * it + b * P, P), :])
            finish(NT, 0, TS, a["y_sample"])
            act.wait_ge(hold_stored, 32)
            act.wait_ge(y_stored[0], 16 * (NT // 2 + 2))
            act.wait_ge(y_stored[1], 16 * (NT // 2 + 1))

        @block.vector
        def _(dve):
            done = [0]

            def chain(ins):
                done[0] += 1
                ins.then_inc(dve_seq, 1)
                dve.wait_ge(dve_seq, done[0])

            dve.sem_inc(w_split, 5)
            dve.sem_inc(c_dve, NV)
            dve.sem_inc(ot_ready, NT + 1)
            dve.wait_ge(tab_loaded, 16)
            dve.tensor_scalar(tabr[0:8, 0:383], tab[0:8, 0:1].to_broadcast([8, 383]), -1.0, None, ALU.mult)\
                .then_inc(tab_ready, 1)
            dve.tensor_scalar(tabr[0:8, 383:767], tab[0:8, 0:384], -1.0, None, ALU.mult).then_inc(tab_ready, 1)
            dve.wait_ge(silu_sig, 1)
            dve.tensor_tensor(cs, col("c", 0, 16), sgc, ALU.mult).then_inc(silu_ready, 1)
            z, s1, s2, acc, lp = (small[:, 4 * i:4 * i + 4] for i in (1, 2, 3, 4, 5))
            dve.wait_ge(sp_a, 2)
            chain(dve.tensor_scalar(s1, z, 2.0, None, ALU.add))
            chain(dve.reciprocal(s2, s1))
            chain(dve.tensor_tensor(s1, z, s2, ALU.mult))
            chain(dve.tensor_tensor(s2, s1, s1, ALU.mult))
            chain(dve.tensor_scalar(acc, s2, 1 / 17.0, 1 / 15.0, ALU.mult, ALU.add))
            for k in (13, 11, 9, 7, 5, 3, 1):
                chain(dve.tensor_tensor(acc, acc, s2, ALU.mult))
                chain(dve.tensor_scalar(acc, acc, 1.0 / k, None, ALU.add))
            chain(dve.scalar_tensor_tensor(lp, acc, 2.0, s1, ALU.mult, ALU.mult))
            chain(dve.tensor_scalar(acc, col("lam", 0, 4), -1.0, 0.0, ALU.mult, ALU.max))
            chain(dve.tensor_tensor(lp, lp, acc, ALU.add))
            dve.tensor_scalar(sp8, lp, 8.0, None, ALU.mult).then_inc(sp_v, 1)

            for g in range(5):
                tiles = range(4 * g, min(4 * g + 4, NT + 1))
                rows = P if g < 4 else TS
                lot = rstd[0:rows, tiles[0]:tiles[-1] + 1]
                dve.wait_ge(ss_ready, tiles[-1] + 1)
                dve.tensor_scalar(lot, lot, 1.0 / D, EPS, ALU.mult, ALU.add).then_inc(var_ready, 1)
                dve.wait_ge(std_ready, g + 1)
                dve.reciprocal(lot, lot).then_inc(rstd_ready, 1)
                dve.wait_ge(rstd_ready, g + 1)
                for i in list(tiles) + [tiles[-1] + 1]:
                    if i in tiles:
                        if i >= 2:
                            dve.wait_ge(xT_filled, i - 1)
                        dve.tensor_scalar(xn[0:rows, i % 2], x_all[0:rows, i, :], rstd[0:rows, i:i + 1], None,
                                          ALU.mult).then_inc(xn_ready, 1)
                    if i > tiles[0]:
                        dve.wait_ge(xT_filled, i)
                        dve.tensor_copy(xT[:, i - 1, 0:4, 0:rows],
                                        ps[:, 2 * ((i - 1) % 2), :].rearrange("p (k t) -> p k t", t=P)[:, :, 0:rows])\
                            .then_inc(xT_dve, 1)

            def coefficients(m):
                g = col("g_mix" if m == 0 else "g_ffn", 0, KT)
                for s in range(2):
                    chain(dve.scalar_tensor_tensor(coefv[:, m, 0, s], modv[:, m, KT:2 * KT, s], 1.0, g,
                                                   ALU.add, ALU.mult))
                    chain(dve.tensor_scalar(coefv[:, m, 0, s], coefv[:, m, 0, s], XS, None, ALU.mult))
                    chain(dve.tensor_scalar(coefv[:, m, 1, s], modv[:, m, 0:KT, s], XS, None, ALU.mult))

            def rows_of(src, m, f0, n):
                c = COLS["mod_b"] + 24 * m + f0
                for s in range(2):
                    ins = dve.tensor_tensor(modv[:, m, f0:f0 + n, s], src.rearrange("p (f s) -> p f s", s=2)[:, :, s],
                                            par[:, c:c + n], ALU.add)
                return ins

            for g in range(2, 4):
                dve.wait_ge(arow_filled, g + 1)
                dve.tensor_copy(arow[0:2, 512 * g:512 * g + 512], ps[0:2, 4 + g, :]).then_inc(arow_dve, 1)
            dve.wait_ge(mod_filled, 1)
            chain(rows_of(ps[:, 0, 0:32], 0, 0, 16))
            coefficients(0)

            def modulate_block(n):
                tiles = slice(4 * n, 4 * n + 4) if n < 4 else slice(NT, NT + 1)
                rows, src = (P, 0) if n < 4 else (TS, 1)
                if n == 0:
                    dve.wait_ge(xT_act, NT + 1)
                    dve.wait_ge(xT_dve, NT + 1)
                for k in range(KT):
                    ins = dve.tensor_scalar(xT[:, tiles, k, 0:rows], xT[:, tiles, k, 0:rows],
                                            coefv[:, 0, 0, src, k:k + 1], coefv[:, 0, 1, src, k:k + 1],
                                            ALU.mult, ALU.add)
                ins.then_inc(modulated, 1)

            def low_block(n):
                for i in range(4 * n, min(4 * n + 4, NT + 1)):
                    rows = P if i < NT else TS
                    dve.wait_ge(hi_ready, i + 1)
                    dve.tensor_tensor(hT[:, :, 1, i * P:i * P + rows], xT[:, i, :, 0:rows],
                                      hT[:, :, 0, i * P:i * P + rows], ALU.subtract).then_inc(hT_ready, 1)

            def split_lo(n, s):
                dve.wait_ge(w_hi, n)
                dve.scalar_tensor_tensor(wsp[:, s, 1], wst[:, s], WS, wsp[:, s, 0], ALU.mult, ALU.subtract)\
                    .then_inc(w_split, 1)

            for n in range(5):
                modulate_block(n)
                if n == 0:
                    split_lo(1, 0)
                low_block(n)
                if n == 1:
                    split_lo(2, 1)

            dve.wait_ge(band_stored, 16)

            with nc.vector.Fori(0, NJ) as j:
                n_chain = [0]

                def step(ins):
                    n_chain[0] += 1
                    ins.then_inc(rg_dve, 1)
                    return n_chain[0]

                def after(n):
                    dve.wait_ge(rg_dve, 10 * j + n)

                dve.wait_ge(gap_ready, 2)
                dve.wait_ge(c_act, NA * j + NA + 5)
                dve.wait_ge(rg_act, 6 * j + 2)
                cw = col("cw", 0, 16).rearrange("p (j w) -> p j w", w=4)
                w_at = lambda n: cw[:, ds(j, 1), n:n + 1].rearrange("p j w -> p (j w)")
                cb, sp8j = col("cb", 0, 4)[:, ds(j, 1)], sp8[:, ds(j, 1)]
                for g, b in enumerate(("ba", "bx")):
                    dve.tensor_copy(gbias[:, g:g + 1], col(b, 0, 4)[:, ds(j, 1)])
                dve.tensor_copy(holdv[:, ds(j, 1), 0:3].rearrange("p j c -> p (j c)"), bufA[:, TP:TP + 3])
                dve.tensor_copy(holdv[:, ds(j, 1), 3:6].rearrange("p j c -> p (j c)"),
                                bufA[:, TP + 3 + TS:TP + 6 + TS])
                dve.tensor_scalar(bufX, bufA[:, 0:LB], w_at(0), cb, ALU.mult, ALU.add).then_inc(xc_ready, 1)
                for n in range(1, 4):
                    dve.wait_ge(xc_ready, 4 * j + n)
                    dve.scalar_tensor_tensor(bufX, bufA[:, n:n + LB], w_at(n), bufX, ALU.mult, ALU.add)\
                        .then_inc(xc_ready, 1)
                split_lo(5 * j + 3, 0)
                split_lo(5 * j + 4, 1)

                def q_lo(n):
                    t, w = BLOCKS[n]
                    u = U_Q + n
                    dve.wait_ge(c_hi, 11 * j + n + 1)
                    for h in range(2):
                        own, other = slice(64 * h, 64 * h + 64), slice(64 - 64 * h, 128 - 64 * h)
                        ins = dve.scalar_tensor_tensor(qs[other, h, t:t + w], ps[own, u % 8, 0:w], -CS * HD ** -0.5,
                                                       qs[own, h, t:t + w], ALU.mult, ALU.subtract)
                    ins.then_inc(c_dve, 1)

                def k_lo(n):
                    if n < 5:
                        t, w = BLOCKS[n]
                        kt, u, sc = (t if t < TP else TP + PAST), U_K + n, CS
                    else:
                        kt, w, u, sc = TP, PAST, U_KC, 1.0
                    dve.wait_ge(c_hi, 11 * j + 5 + n + 1)
                    for h in range(2):
                        own = slice(64 * h, 64 * h + 64)
                        ins = dve.scalar_tensor_tensor(kll[own, h, kt:kt + w], ps[own, u % 8, 0:w], sc,
                                                       khh[own, h, kt:kt + w], ALU.mult, ALU.subtract)
                    ins.then_inc(c_dve, 1)
                    dve.wait_ge(c_dve, NV * j + NV + 5 + n + 1)
                    for h in range(2):
                        own, other = slice(64 * h, 64 * h + 64), slice(64 - 64 * h, 128 - 64 * h)
                        dve.tensor_copy(khh[other, h, kt:kt + w], khh[own, h, kt:kt + w])
                        ins = dve.tensor_copy(kll[other, h, kt:kt + w], kll[own, h, kt:kt + w])
                    ins.then_inc(kdup, 1)

                def v_out(b):
                    u = U_V + b
                    dve.wait_ge(c_filled, NU * j + NU + u + 1)
                    if b < 4:
                        dve.tensor_scalar(vv[:, 4 * b:4 * b + 4, :],
                                          ps[:, u % 8, :].rearrange("p (i d) -> p i d", d=P), CS, None, ALU.mult)\
                            .then_inc(c_dve, 1)
                    else:
                        dve.tensor_scalar(vv[0:TS, NT + 4, :], ps[0:TS, u % 8, 0:P], CS, None, ALU.mult)\
                            .then_inc(c_dve, 1)

                for n in range(5):
                    q_lo(n)
                split_lo(5 * j + 5, 0)
                dve.wait_ge(c_act, NA * j + NA + 20)
                step(dve.memset(bufA[:, TP:TP + 3], 0.0))
                after(1)
                step(dve.tensor_scalar(bufA[:, 0:LB], bufA[:, 0:LB], sp8j, None, ALU.mult))
                k_lo(0)
                k_lo(1)
                dve.wait_ge(rg_act, 6 * j + 3)
                dve.wait_ge(rnn_stored, 32 * j + 32)
                step(dve.tensor_scalar(bufR, bufT, 1.0, None, ALU.add))
                after(3)
                step(dve.reciprocal(bufR, bufR))
                after(4)
                step(dve.scalar_tensor_tensor(bufT, bufT, 2.0, bufR, ALU.mult, ALU.mult))
                k_lo(2)
                k_lo(3)
                step(dve.tensor_tensor(bufI, bufI, bufX, ALU.mult))
                k_lo(4)
                k_lo(5)
                dve.wait_ge(rg_act, 6 * j + 5)
                after(6)
                step(dve.tensor_tensor(bufI, bufI, bufT, ALU.mult))
                dve.wait_ge(v_stored, 32 * j + 32)
                v_out(0)
                after(7)
                dve.tensor_tensor_scan(bufX[:, 0:TP], bufA[:, 0:TP], bufI[:, 0:TP], 0.0, ALU.mult, ALU.add)
                step(dve.tensor_tensor_scan(bufX[:, TP + 3:LB], bufA[:, TP + 3:LB], bufI[:, TP + 3:LB],
                                            col("h0", 0, 4)[:, ds(j, 1)], ALU.mult, ALU.add))
                v_out(1)
                after(8)
                dve.tensor_copy(holdv[:, ds(j, 1), 6:7].rearrange("p j c -> p (j c)"), bufX[:, TP - 1:TP])
                dve.tensor_copy(holdv[:, ds(j, 1), 7:8].rearrange("p j c -> p (j c)"), bufX[:, LB - 1:LB])\
                    .then_inc(held, 1)
                dve.wait_ge(held, j + 1)
                step(dve.tensor_tensor(bufX, bufX, bufG, ALU.mult))
                v_out(2)
                dve.wait_ge(rg_act, 6 * j + 6)
                after(9)
                step(dve.scalar_tensor_tensor(rstage[:, 1, :], bufX, XS, rstage[:, 0, :], ALU.mult, ALU.subtract))
                v_out(3)
                v_out(4)
                dve.wait_ge(aux_loaded, 16 * j + 16)
                dve.memset(bias[0:64, :, BAND - 64:BAND], MASKED)
                dve.memset(bias[64:128, :, 0:64], MASKED).then_inc(bias_masked, 1)
                dve.wait_ge(bias_masked, j + 1)

                def scores(n, h, rows, w, b0, old):
                    dve.wait_ge(s_filled, n)
                    if old is not None:
                        dve.wait_ge(t_filled, old)
                    if w > 512:
                        src = ps[0:rows, 2 * h:2 * h + 2, :].rearrange("p b n -> p (b n)")[:, 0:w]
                    else:
                        src = ps[0:rows, 2 * h, 0:w]
                    dve.memset(mark[:, h:h + 1], 0.0)
                    dve.tensor_tensor_reduce(pr[0:rows, h, 0:w], src, bias[0:rows, h, b0:b0 + w], 1.0, 3.0e38,
                                             ALU.add, ALU.min, least[0:rows, h:h + 1]).then_inc(s_added, 1)

                def probs(n, h, rows, w, first=False):
                    if not first:
                        dve.wait_ge(o_ready, n - 2)
                    dve.wait_ge(p_ready, n)
                    dve.reciprocal(rs[0:rows, h:h + 1], sm[0:rows, h:h + 1]).then_inc(r_ready, 1)
                    if w > 512:
                        k = min(P, w - 512)
                        dve.wait_ge(t_filled, n)
                        dve.tensor_copy(pt[0:k, h, 4 * P:5 * P], ps[0:k, 5, 0:P]).then_inc(t_dve, 1)

                def out_n(n, h, rows, ot):
                    dve.wait_ge(o_filled, n)
                    dve.wait_ge(r_ready, n)
                    if ot is not None:
                        dve.wait_ge(ot_filled, ot)
                    dve.tensor_scalar(osb[0:rows, 64 * h:64 * h + 64], ps[0:rows, 6, 64 * h:64 * h + 64],
                                      rs[0:rows, h:h + 1], None, ALU.mult).then_inc(o_ready, 1)

                def out_lo(n, t, w):
                    dve.wait_ge(ot_hi, n)
                    dve.scalar_tensor_tensor(ost[:, 1, ds(t, w)], ps[:, 7, 0:w], XS, ost[:, 0, ds(t, w)],
                                             ALU.mult, ALU.subtract).then_inc(ot_ready, 1)

                un = NUNIT * j
                tn = (NT + 1) * j
                for p in range(5):
                    w, pw = min(BAND, P * (p + 1)), min(BAND, P * p)
                    if p == 3:
                        split_lo(5 * j + 6, 0)
                        split_lo(5 * j + 7, 1)
                    for h in range(2):
                        scores(un + 2 * p + h + 1, h, P, w, BAND - w, un + 2 * p + h - 1 if p else None)
                        if p or h:
                            probs(un + 2 * p + h, 1 - h, P, w if h else pw, 2 * p + h < 3)
                        if p:
                            out_n(un + 2 * p + h - 1, h, P, tn + p - 1 if p >= 2 and h == 0 else None)
                        if h == 0 and p >= 2:
                            out_lo(tn + p - 1, (p - 2) * P, P)
                with nc.vector.Fori(5, NT) as p:
                    for h in range(2):
                        scores(un + 2 * p + h + 1, h, P, BAND, 0, un + 2 * p + h - 1)
                        probs(un + 2 * p + h, 1 - h, P, BAND)
                        out_n(un + 2 * p + h - 1, h, P, tn + p - 1 if h == 0 else None)
                        if h == 0:
                            out_lo(tn + p - 1, (p - 2) * P, P)
                scores(un + 2 * NT + 1, 0, TS, PAST + TS, 0, un + 2 * NT - 1)
                probs(un + 2 * NT, 1, P, BAND)
                out_n(un + 2 * NT - 1, 0, P, tn + NT - 1)
                out_lo(tn + NT - 1, (NT - 2) * P, P)
                scores(un + 2 * NT + 2, 1, TS, PAST + TS, 0, un + 2 * NT)
                probs(un + 2 * NT + 1, 0, TS, PAST + TS)
                out_n(un + 2 * NT, 1, P, None)
                probs(un + 2 * NT + 2, 1, TS, PAST + TS)
                out_lo(tn + NT, (NT - 1) * P, P)
                out_n(un + 2 * NT + 1, 0, TS, tn + NT)
                out_n(un + 2 * NT + 2, 1, TS, None)
                out_lo(tn + NT + 1, TP, TS)

            dve.sem_inc(d_dve, 4)
            dve.sem_inc(dm_used, 1)
            dve.sem_inc(d_split, 3)

            def merge_lo(it, q):
                for i in range(3):
                    dve.wait_ge(d_hi, 6 * it + 3 * q + i + 1)
                    dve.scalar_tensor_tensor(dsp[:, 3 * q + i, 1], dst[:, i], WS, dsp[:, 3 * q + i, 0],
                                             ALU.mult, ALU.subtract).then_inc(d_split, 1)

            def merge_body(it, last):
                for q in range(2):
                    for n, (t, w) in enumerate(BLOCKS):
                        g, b = 10 * it + 5 * q + n, (5 * q + n) % 2
                        for m in range(2):
                            dve.wait_ge(d_filled, 40 + 4 * g + m + 3)
                            dve.wait_ge(d_act, 4 + 2 * g + m + 1)
                            dve.scalar_tensor_tensor(sig[:, b, m, 0:w], ps[:, 4 * b + 2 + m, 0:w], 1.0 / WS,
                                                     sig[:, b, m, 0:w], ALU.mult, ALU.mult).then_inc(d_dve, 1)
                        dve.wait_ge(d_dve, 4 + 2 * g + 2)
                        dve.tensor_tensor(mrg[:, b, 0:w], sig[:, b, 0, 0:w], sig[:, b, 1, 0:w], ALU.add)\
                            .then_inc(d_step, 1)
                        dve.wait_ge(d_mhi, g + 1)
                        dve.tensor_tensor(mstage[:, 1, t:t + w], mrg[:, b, 0:w], mstage[:, 0, t:t + w],
                                          ALU.subtract).then_inc(d_mlo, 1)
                        if n == 1 and not (last and q == 1):
                            merge_lo(it + q, 1 - q)
                        if last and q == 1 and n == 4:
                            for k in range(3):
                                out_lo_part(k)
                        if n < 4:
                            adaln_tile(it, 4 * q + n)
                dve.wait_ge(dm_step, 16 * it + 17)
                dve.tensor_copy(modraw[:, ds(16 * it, 16)], dsum).then_inc(dm_kept, 1)

            def out_lo_part(k):
                dve.wait_ge(e_whi, k + 1)
                dve.scalar_tensor_tensor(wo[:, k, 1, :], est[k], WS, wo[:, k, 0, :], ALU.mult, ALU.subtract)\
                    .then_inc(e_split, 1)

            def adaln_tile(it, i):
                n = 8 * it + i
                if i == 0:
                    dve.wait_ge(dm_kept, it + 1)
                dve.wait_ge(dmw_loaded, 16 * n + 16)
                for s in range(2):
                    dve.wait_ge(dm_step, 2 * n + s + 1)
                    ins = dve.tensor_tensor_reduce(djunk, dmw, crow[:, s, :], 1.0, 0.0, ALU.mult, ALU.add,
                                                   dsum[:, 2 * i + s:2 * i + s + 1])
                    ins.then_inc(dm_step, 1)
                dve.wait_ge(dm_step, 2 * n + 3)
                dve.sem_inc(dm_used, 1)

            dve.sem_inc(dm_step, 1)
            dve.sem_inc(dm_kept, 1)
            merge_lo(0, 0)
            dve.wait_ge(crow_sig, 1)
            dve.tensor_tensor(crow_, crow_, sig_, ALU.mult).then_inc(crow_ready, 1)
            dve.wait_ge(crow_ready, 1)
            with nc.vector.Fori(0, KT // 2 - 1) as it:
                merge_body(it, False)
            dve.wait_ge(dm_kept, 2)
            chain(rows_of(modraw[:, 0:16], 0, 16, 8))
            dve.sem_inc(gate_ready, 1)
            merge_body(KT // 2 - 1, True)
            dve.wait_ge(dm_kept, 1 + KT // 2)
            chain(rows_of(modraw[:, 16:64], 1, 0, 24))
            coefficients(1)
            dve.sem_inc(gate_ready, 1)

            dve.sem_inc(e_evac, 2)
            dve.sem_inc(e_tmp, 3)
            for k in range(3, KT):
                out_lo_part(k)

            def residual(i, b, rows, src, nx, sems, xbuf, gates):
                filled, loaded, gated, evac = sems
                dve.wait_ge(filled, i + 1)
                out = ps[0:rows, 2 * b:2 * b + 2, :].rearrange("p b n -> p (b n)")
                dve.scalar_tensor_tensor(out, out, CS, gates[0:rows, src, :], ALU.mult, ALU.mult).then_inc(gated, 1)
                dve.wait_ge(loaded[b], 16 * nx)
                dve.wait_ge(gated, i + 1)
                dve.tensor_tensor(xbuf[0:rows, b], out, xbuf[0:rows, b], ALU.add).then_inc(evac, 1)

            def variance(i, b, rows, sems):
                ss, var, std, rst = sems
                dve.wait_ge(ss, i + 1)
                dve.tensor_scalar(rstd[0:rows, b:b + 1], rstd[0:rows, b:b + 1], 1.0 / D, EPS, ALU.mult, ALU.add)\
                    .then_inc(var, 1)
                dve.wait_ge(std, i + 1)
                dve.reciprocal(rstd[0:rows, 4 + b:5 + b], rstd[0:rows, 2 + b:3 + b]).then_inc(rst, 1)

            def modulate2(i, b, rows, src):
                for q in range(2):
                    if q == 0:
                        dve.wait_ge(e_xt, i + 3)
                    for k in range(4 * q, 4 * q + 4):
                        ins = dve.tensor_scalar(etmp[:, b, k, 0:rows],
                                                ps[:, 4 + 2 * b + q, (k % 4) * P:(k % 4) * P + rows],
                                                coefv[:, 1, 0, src, k:k + 1], coefv[:, 1, 1, src, k:k + 1],
                                                ALU.mult, ALU.add)
                    ins.then_inc(e_tmp, 1)

            def low2(i, b, rows):
                for q in range(2):
                    dve.wait_ge(e_hi, 2 * i + q + 1)
                    k = slice(4 * q, 4 * q + 4)
                    dve.tensor_tensor(hT[:, k, 1, ds(i * P, rows)], etmp[:, b, k, 0:rows],
                                      hT[:, k, 0, ds(i * P, rows)], ALU.subtract).then_inc(e_hT, 1)

            E1, E2 = (e_filled, ex_loaded, e_gated, e_evac), (e_ss, e_var, e_std, e_rstd)
            dve.wait_ge(gate1_loaded, 32)
            residual(0, 0, P, 0, 1, E1, ex, gate1)
            variance(0, 0, P, E2)
            with nc.vector.Fori(0, NT // 2 - 1) as it:
                for b in range(2):
                    i = 2 * it + 1 + b
                    residual(i, 1 - b, P, 0, it + 1 + b, E1, ex, gate1)
                    modulate2(2 * it + b, b, P, 0)
                    variance(i, 1 - b, P, E2)
                    low2(2 * it + b, b, P)
            residual(NT - 1, 1, P, 0, NT // 2, E1, ex, gate1)
            modulate2(NT - 2, 0, P, 0)
            variance(NT - 1, 1, P, E2)
            low2(NT - 2, 0, P)
            residual(NT, 0, TS, 1, NT // 2 + 1, E1, ex, gate1)
            modulate2(NT - 1, 1, P, 0)
            variance(NT, 0, TS, E2)
            low2(NT - 1, 1, P)
            modulate2(NT, 0, TS, 1)
            low2(NT, 0, TS)

            dve.sem_inc(f_split, 3)
            dve.sem_inc(f_conv, 1)

            def up_lo(n, s):
                dve.wait_ge(f_hi, n)
                dve.scalar_tensor_tensor(fsp[:, s, 1].rearrange("p k m -> p (k m)"), fst[:, s], WS,
                                         fsp[:, s, 0].rearrange("p k m -> p (k m)"), ALU.mult, ALU.subtract)\
                    .then_inc(f_split, 1)

            def ffn_conv(f, s, out):
                dve.wait_ge(f_act, 10 * f + 10 + 5 * s + 5)
                dve.wait_ge(f_pad, 2 * f + s + 2)
                w3 = col("fw", 0, 132).rearrange("p (f c) -> p f c", c=3)[:, ds(f + NF * s, 1), :]
                tap = lambda n: w3[:, :, n:n + 1].rearrange("p a c -> p (a c)")
                fb = col("fb", 0, 44)[:, ds(f + NF * s, 1)]
                hold = fholdv[:, ds(f + NF * s, 1), :].rearrange("p f c -> p (f c)")
                dve.tensor_copy(hold[:, 0:2], ubuf[:, TP:TP + 2])
                dve.tensor_copy(hold[:, 2:4], ubuf[:, LF:LF + 2])
                dve.tensor_scalar(out, ubuf[:, 0:LF], tap(0), fb, ALU.mult, ALU.add).then_inc(f_conv, 1)
                for n in (1, 2):
                    dve.wait_ge(f_conv, 6 * f + 3 * s + n + 1)
                    dve.scalar_tensor_tensor(out, ubuf[:, n:n + LF], tap(n), out, ALU.mult, ALU.add)\
                        .then_inc(f_conv, 1)

            def ffn_body(f, last):
                up_lo(3 * f + 2, 1)
                dve.wait_ge(f_plo, f + 1)
                ffn_conv(f, 0, yval)
                dve.wait_ge(f_hi, 3 * f + 3)
                dve.scalar_tensor_tensor(wd[:, ds(f, 1), 1, :].rearrange("p k m -> p (k m)"), fst[:, 0], WS,
                                         wd[:, ds(f, 1), 0, :].rearrange("p k m -> p (k m)"),
                                         ALU.mult, ALU.subtract).then_inc(f_split, 1)
                if not last:
                    up_lo(3 * f + 4, 0)
                ffn_conv(f, 1, ygate)
                dve.wait_ge(f_gelu, f + 1)
                dve.scalar_tensor_tensor(yval, yval, XS, ygate, ALU.mult, ALU.mult).then_inc(f_prod, 1)
                dve.wait_ge(f_phi, f + 1)
                dve.tensor_tensor(hstage[:, 1, :], yval, hstage[:, 0, :], ALU.subtract).then_inc(f_plo, 1)

            up_lo(1, 0)
            dve.sem_inc(f_plo, 1)
            with nc.vector.Fori(0, NF - 1) as f:
                ffn_body(f, False)
            ffn_body(NF - 1, True)

            dve.sem_inc(g_evac, 2)
            G1, G2 = (g_filled, gx_loaded, g_gated, g_evac), (g_ss, g_var, g_std, g_rstd)

            def finish(i, b, rows, src, nx):
                residual(i, b, rows, src, nx, G1, gx, gate2)
                variance(i, b, rows, G2)
                dve.wait_ge(g_rstd, i + 1)
                dve.scalar_tensor_tensor(gx[0:rows, b], gx[0:rows, b], rstd[0:rows, 4 + b:5 + b], gfin[0:rows, :],
                                         ALU.mult, ALU.mult).then_inc(g_y, 1)

            dve.wait_ge(rows_loaded, 48)
            with nc.vector.Fori(0, NT // 2) as it:
                for b in range(2):
                    finish(2 * it + b, b, P, 0, it + 1)
            finish(NT, 0, TS, 1, NT // 2 + 1)

        @block.tensor
        def _(pe):
            pe.wait_ge(ident_ready, 2)

            def rows_up(i):
                rows = P if i < NT else TS
                pe.wait_ge(xn_ready, i + 1)
                if i >= 2:
                    pe.wait_ge(xT_act, i - 1)
                    pe.wait_ge(xT_dve, i - 1)
                for k in range(KT):
                    mm = pe.transpose(ps[:, 2 * (i % 2) + k // 4, (k % 4) * P:(k % 4) * P + rows],
                                      xn[0:rows, i % 2, k * P:(k + 1) * P], ident[0:rows, 0:rows])
                mm.then_inc(xT_filled, 1)

            def adaln_rows(g):
                if g == 0:
                    pe.wait_ge(silu_ready, 1)
                pe.wait_ge(mw_loaded[g], 16)
                for k in range(KT):
                    mm = pe.matmul(ps[0:2, 4 + g, :], csv[:, k, :], mw[:, 4 * g:4 * g + 4, k, :],
                                   start=(k == 0), stop=(k == KT - 1))
                mm.then_inc(arow_filled, 1)

            for i in range(NT + 1):
                rows_up(i)
                if i == 11:
                    adaln_rows(0)
                if i == 15:
                    adaln_rows(1)
            adaln_rows(2)
            adaln_rows(3)
            pe.wait_ge(arow_act, 2)
            pe.wait_ge(arow_dve, 2)
            for f in range(16):
                mm = pe.transpose(ps[:, 0, 2 * f:2 * f + 2], arow[0:2, f * P:(f + 1) * P], ident[0:2, 0:2])
            mm.then_inc(mod_filled, 1)

            pe.sem_inc(c_filled, NU)
            with nc.tensor.Fori(0, NJ) as j:
                def bank(u):
                    if u >= 8:
                        e, n = drained_before(u - 8)
                        if e == "A":
                            pe.wait_ge(c_act, NA * j + NA + n)
                        else:
                            pe.wait_ge(c_dve, NV * j + NV + n)
                    return ps[:, u % 8, :]

                def unit(u0, s):
                    for n, (t, w) in enumerate(BLOCKS):
                        out = bank(u0 + n)
                        if u0 == U_RX:
                            pe.wait_ge(hT_ready, min(4 * n + 4, NT + 1))
                        for k in range(KT):
                            for m, (wp, hp) in enumerate(PASSES):
                                mm = pe.matmul(out[:, 0:w], wsp[:, s, wp, k, :], hT[:, k, hp, t:t + w],
                                               start=(k == 0 and m == 0), stop=(k == KT - 1 and m == 2))
                        mm.then_inc(c_filled, 1)

                pe.wait_ge(ot_ready, (NT + 1) * (j + 1))
                pe.wait_ge(w_split, 5 * j + 6)
                unit(U_RX, 0)
                pe.wait_ge(w_split, 5 * j + 7)
                unit(U_RG, 1)
                pe.wait_ge(w_split, 5 * j + 8)
                unit(U_Q, 0)
                pe.wait_ge(xc_ready, 4 * j + 4)
                pe.wait_ge(gw_loaded, 32 * j + 32)
                for n, (t, w) in enumerate(BLOCKS):
                    o = 0 if t < TP else 3
                    for g in range(2):
                        out = bank(U_G + 2 * n + g)
                        pe.matmul(out[:, 0:w], gw[:, g, :], bufX[:, t + o:t + o + w], start=True, stop=True)\
                            .then_inc(c_filled, 1)
                pe.wait_ge(w_split, 5 * j + 9)
                unit(U_K, 1)
                pe.wait_ge(kc_loaded, 16 * j + 16)
                out = bank(U_KC)
                for c in range(4):
                    mm = pe.transpose(out[:, c * P:(c + 1) * P], kc[:, c, :], ident)
                mm.then_inc(c_filled, 1)
                pe.wait_ge(w_split, 5 * j + 10)
                for i in range(NT + 1):
                    rows = P if i < NT else TS
                    if i % 4 == 0:
                        out = bank(U_V + i // 4)
                    for k in range(KT):
                        for m, (wp, hp) in enumerate(PASSES):
                            mm = pe.matmul(out[0:rows, (i % 4) * P:(i % 4) * P + P],
                                           hT[:, k, hp, i * P:i * P + rows], wsp[:, 0, wp, k, :],
                                           start=(k == 0 and m == 0), stop=(k == KT - 1 and m == 2))
                    if i % 4 == 3 or i == NT:
                        mm.then_inc(c_filled, 1)

                def scores(n, h, q0, rows, k0, w):
                    if n is not None:
                        pe.wait_ge(s_added, n)
                    for b, c in ((0, min(w, 512)), (1, w - 512)):
                        if c <= 0:
                            continue
                        for m, kk in enumerate((khh, kll)):
                            mm = pe.matmul(ps[0:rows, 2 * h + b, 0:c], qs[:, h, ds(q0, rows)],
                                           kk[:, h, ds(k0 + 512 * b, c)], start=(m == 0), stop=(m == 1))
                    mm.then_inc(s_filled, 1)

                def probs(n, h, rows, w, ta, td):
                    pe.wait_ge(p_ready, n)
                    if ta is not None:
                        pe.wait_ge(t_act, ta)
                    if td is not None:
                        pe.wait_ge(t_dve, td)
                    for c in range((w + P - 1) // P):
                        k = min(P, w - c * P)
                        mm = pe.transpose(ps[0:k, 4 + c // 4, (c % 4) * P:(c % 4) * P + P],
                                          pr[:, h, c * P:c * P + k], ident)
                    mm.then_inc(t_filled, 1)

                def outs(n, h, rows, v0, w, td, on):
                    pe.wait_ge(t_act, n)
                    if td is not None:
                        pe.wait_ge(t_dve, td)
                    if on is not None:
                        pe.wait_ge(o_ready, on)
                    nk = (w + P - 1) // P
                    for c in range(nk):
                        k = min(P, w - c * P)
                        mm = pe.matmul(ps[0:rows, 6, 64 * h:64 * h + 64], pt[0:k, h, c * P:c * P + rows],
                                       vv[0:k, ds(v0 + c, 1), 64 * h:64 * h + 64].rearrange("p a d -> p (a d)"),
                                       start=(c == 0), stop=(c == nk - 1))
                    mm.then_inc(o_filled, 1)

                def out_t(n, rows, hi):
                    pe.wait_ge(o_ready, 2 * n)
                    if hi is not None:
                        pe.wait_ge(ot_ready, hi)
                    pe.transpose(ps[:, 7, 0:P], osb, ident).then_inc(ot_filled, 1)

                un = NUNIT * j
                tn = (NT + 1) * j
                full = 2 * (NT - 4) + 2
                tdn = full * j
                pe.wait_ge(kdup, 6 * j + 6)
                pe.wait_ge(c_dve, NV * j + 2 * NV)
                pe.wait_ge(c_act, NA * j + 2 * NA)
                pe.wait_ge(v_loaded, 16 * j + 16)

                def td_of(unit):
                    n = max(0, unit - 7)
                    return tdn + n if n > 0 else None

                ws = PAST + TS
                scores(None, 0, 0, P, 0, P)
                for p in range(5):
                    w, pw = min(BAND, P * (p + 1)), min(BAND, P * p)
                    for h in range(2):
                        i = 2 * p + h
                        nxt = p + h
                        scores(un + i if i >= 1 else None, 1 - h, nxt * P, P, max(0, nxt - 4) * P,
                               min(BAND, P * (nxt + 1)))
                        if h == 0 and p >= 2:
                            out_t(tn + p - 1, P, tn + p + NT - 1 if p > 2 else None)
                        if i >= 1:
                            probs(un + i, 1 - h, P, w if h else pw, un + i - 1 if i >= 2 else None, td_of(i - 2))
                        if i >= 2:
                            outs(un + i - 1, h, P, 0, pw, td_of(i - 2), un + i - 2 if i >= 3 else None)

                def full_tile(p, last):
                    for h in range(2):
                        i = 2 * p + h
                        if h and last:
                            scores(un + i, 0, TP, TS, TP, ws)
                        else:
                            scores(un + i, 1 - h, (p + h) * P, P, (p + h - 4) * P, BAND)
                        if h == 0:
                            out_t(tn + p - 1, P, tn + p + NT - 1)
                        probs(un + i, 1 - h, P, BAND, un + i - 1, tdn + i - 9)
                        outs(un + i - 1, h, P, p - 5, BAND, tdn + i - 9, un + i - 2)

                with nc.tensor.Fori(5, NT - 1) as p:
                    full_tile(p, False)
                full_tile(NT - 1, True)
                i = 2 * NT
                scores(un + i, 1, TP, TS, TP, ws)
                out_t(tn + NT - 1, P, tn + 2 * NT - 1)
                probs(un + i, 1, P, BAND, un + i - 1, tdn + i - 9)
                outs(un + i - 1, 0, P, NT - 5, BAND, tdn + i - 9, un + i - 2)
                i += 1
                probs(un + i, 0, TS, ws, un + i - 1, tdn + i - 9)
                outs(un + i - 1, 1, P, NT - 5, BAND, tdn + i - 9, un + i - 2)
                i += 1
                probs(un + i, 1, TS, ws, un + i - 1, tdn + i - 9)
                out_t(tn + NT, P, tn + 2 * NT)
                outs(un + i - 1, 0, TS, NT, ws, tdn + i - 9, un + i - 2)
                i += 1
                outs(un + i - 1, 1, TS, NT, ws, tdn + i - 9, un + i - 2)
                out_t(tn + NT + 1, TS, tn + 2 * NT + 1)

            pe.sem_inc(d_filled, 40)
            pe.wait_ge(ot_ready, (NT + 1) * (NJ + 1))

            def product(out, w, k0, k1, wt, act_t, t, sem_):
                for k in range(k0, k1):
                    for m, (wp, hp) in enumerate(PASSES):
                        mm = pe.matmul(out, wt[:, wp, k, :], act_t[:, k, hp, t:t + w],
                                       start=(k == k0 and m == 0), stop=(k == k1 - 1 and m == 2))
                mm.then_inc(sem_, 1)

            with nc.tensor.Fori(0, KT // 2) as it:
                for q in range(2):
                    pe.wait_ge(d_split, 6 * it + 3 * q + 6)
                    for n, (t, w) in enumerate(BLOCKS):
                        g, b = 10 * it + 5 * q + n, (5 * q + n) % 2
                        pe.wait_ge(d_act, 2 * g + 2)
                        pe.wait_ge(d_dve, 2 * g + 2)
                        for m in range(2):
                            product(ps[:, 4 * b + m, 0:w], w, 0, KT, dsp[:, 3 * q + m], hT, t, d_filled)
                        pe.wait_ge(mix_loaded, 16 * KT)
                        for m in range(2):
                            product(ps[:, 4 * b + 2 + m, 0:w], w, 4 * m, 4 * m + 4, dsp[:, 3 * q + 2], mixT, t,
                                    d_filled)

            pe.sem_inc(e_xt, 2)
            pe.wait_ge(d_dve, 4 + 10 * KT)
            pe.wait_ge(e_split, KT)

            def project(i, b, rows, ev):
                pe.wait_ge(e_evac, i + 1)
                for m in range(2):
                    for k in range(KT):
                        for n, (wp, hp) in enumerate(PASSES):
                            mm = pe.matmul(ps[0:rows, 2 * b + m, :], mT[:, k, hp, ds(i * P, rows)],
                                           wo[:, k, wp, 512 * m:512 * m + 512],
                                           start=(k == 0 and n == 0), stop=(k == KT - 1 and n == 2))
                mm.then_inc(e_filled, 1)

            def transposes2(i, b, rows):
                pe.wait_ge(e_xn, i + 1)
                pe.wait_ge(e_tmp, 2 * i + 1)
                for k in range(KT):
                    mm = pe.transpose(ps[:, 4 + 2 * b + k // 4, (k % 4) * P:(k % 4) * P + rows],
                                      exn[0:rows, b, k * P:(k + 1) * P], ident[0:rows, 0:rows])
                mm.then_inc(e_xt, 1)

            pe.wait_ge(m_loaded[0], 32)
            project(0, 0, P, None)
            for n, lo, hi in ((0, 0, 1), (1, 1, 3), (2, 3, 5), (3, 5, 7)):
                pe.wait_ge(m_loaded[n], 32)
                with nc.tensor.Fori(lo, hi) as it:
                    for b in range(2):
                        project(2 * it + 1 + b, 1 - b, P, None)
                        transposes2(2 * it + b, b, P)
            pe.wait_ge(m_loaded[4], 32)
            project(NT - 1, 1, P, None)
            transposes2(NT - 2, 0, P)
            project(NT, 0, TS, None)
            transposes2(NT - 1, 1, P)
            transposes2(NT, 0, TS)

            pe.sem_inc(f_filled, 10)
            pe.wait_ge(e_hT, 2 * (NT + 1))
            with nc.tensor.Fori(0, NF) as f:
                for s in range(2):
                    pe.wait_ge(f_split, 3 * f + s + 4)
                    for n, (t, w) in enumerate(BLOCKS):
                        u = 5 * s + n
                        pe.wait_ge(f_act, 10 * f + (u + 3 if u >= 8 else u + 9 if u < 2 else u + 1))
                        product(ps[:, u % 8, 0:w], w, 0, KT, fsp[:, s], hT, t, f_filled)

            pe.wait_ge(f_act, 10 * NF + 10)
            pe.wait_ge(f_split, 3 * NF + 3)

            def down(i, b, rows, blk, t, last=None):
                pe.wait_ge(g_evac, i + 1)
                for m in range(2):
                    for k in range(NF):
                        if k == NF - 1 and last is not None:
                            pe.wait_ge(last, 32)
                        for n, (wp, hp) in enumerate(PASSES):
                            mm = pe.matmul(ps[0:rows, 2 * b + m, :], hb[blk][:, k, hp, t:t + rows],
                                           wd[:, k, wp, 512 * m:512 * m + 512],
                                           start=(k == 0 and n == 0), stop=(k == NF - 1 and n == 2))
                mm.then_inc(g_filled, 1)

            with nc.tensor.Fori(0, 2) as ib:
                for s in range(2):
                    for q in range(2):
                        pe.wait_ge(hb_loaded[s][q], 32 * ib + 32)
                        for b in range(2):
                            down(8 * ib + 4 * s + 2 * q + b, b, P, s, 256 * q + 128 * b,
                                 hb_last[q] if s == 0 else None)
            pe.wait_ge(hs_loaded, 32)
            down(NT, 0, TS, 0, 0)


_IN = [("params", (P, NPAR)), ("rel_table", (8, 513)), ("x_prompt", (TP, D)), ("x_sample", (TS, D)),
       ("w_mod", (16, P, KT, P)), ("w_mod_rest", (32, P, D)), ("c", (2, D)), ("w_in", (36, P, KT, P)), ("cache_k", (4, P, NJ, P)), ("cache_v", (4, P, NJ, P)),
       ("w_rgate", (2, 8, 64, 64)), ("w_branch", (KT, P, KT, P)), ("w_out", (KT, P, D)), ("w_up", (2 * NF, P, KT, P)),
       ("w_down", (NF, P, D)), ("g_final", (1, D))]
_OUT = [("k_prompt", (NJ, P, PAST)), ("k_sample", (NJ, P, TS)), ("v_prompt", (4, P, NJ, P)),
        ("v_sample", (TS, NJ, P)), ("rnn_hold", (P, 32)), ("y_prompt", (TP, D)), ("y_sample", (TS, D)),
        ("ffn_hold", (P, 176))]


def declare(nc):
    a = {}
    for name, shape in _IN:
        a[name] = nc.dram_tensor(f"in_{name}", shape, F32, kind="ExternalInput").ap()
    for name, shape in _OUT:
        a[name] = nc.dram_tensor(f"out_{name}", shape, F32, kind="ExternalOutput").ap()
    return a


def lay_out(i):
    import numpy as np

    def tiles(w):
        k, m = w.shape
        return np.ascontiguousarray(w.reshape(k // P, P, m // P, P).transpose(2, 1, 0, 3))

    def cols(v):
        v = np.asarray(v)
        v = v.reshape(v.shape[:-1] + (v.shape[-1] // P, P))
        return np.moveaxis(v, (-1, -2), (0, 1)).reshape(P, -1)

    c = np.concatenate([i["c_prompt"], i["c_sample"]])
    par = [cols(c), cols(i["mod_mix_b"][0]), cols(i["mod_ffn_b"][0]), cols(i["norm_mix_g"][0]),
           cols(i["norm_ffn_g"][0]), cols(i["rnn_conv_w"][0]), cols(i["rnn_conv_b"][0]), cols(i["rnn_gate_a_b"][0]),
           cols(i["rnn_gate_x_b"][0]), cols(i["rnn_lambda"][0]), cols(i["state_rnn_h"][0, 0]),
           cols(i["state_rnn_conv"][0, 0]), cols(i["ffn_conv_w"][0]), cols(i["ffn_conv_b"][0]),
           cols(i["state_ffn_conv"][0, 0])]
    return {
        "params": np.ascontiguousarray(np.concatenate(par, axis=1)),
        "rel_table": np.ascontiguousarray(i["rel_bias_table"][0].T[:, ::-1]),
        "x_prompt": np.ascontiguousarray(i["x_prompt"][0]),
        "x_sample": np.ascontiguousarray(i["x_sample"][0]),
        "c": c,
        "w_mod": tiles(i["mod_mix_w"][0][:, 0:2 * D]),
        "w_mod_rest": np.concatenate([i["mod_mix_w"][0][:, 2 * D:3 * D].T, i["mod_ffn_w"][0].T]).reshape(32, P, D),
        "w_in": tiles(i["w_in"][0]),
        "cache_k": np.ascontiguousarray(i["cache_k"].reshape(4, P, NJ, P)),
        "cache_v": np.ascontiguousarray(i["cache_v"].reshape(4, P, NJ, P)),
        "w_rgate": np.stack([i["rnn_gate_a_w"][0], i["rnn_gate_x_w"][0]]),
        "w_branch": tiles(i["w_branch"][0]),
        "w_out": np.ascontiguousarray(i["w_out"][0].reshape(KT, P, D)),
        "w_up": tiles(i["ffn_up_w"][0]),
        "w_down": np.ascontiguousarray(i["ffn_down_w"][0].reshape(NF, P, D)),
        "g_final": i["final_norm_g"][None],
    }


def kernel(**inputs):
    import numpy as np
    import concourse.bacc as bacc
    from concourse.bass_utils import run_bass_kernel_spmd

    nc = bacc.Bacc("TRN2", target_bir_lowering=False, num_devices=1)
    a = declare(nc)
    build(nc, a)
    arrays = {f"in_{k}": v for k, v in lay_out({k: np.asarray(v) for k, v in inputs.items()}).items()}
    got = run_bass_kernel_spmd(nc, [arrays], core_ids=[0]).results[0]
    out = {name: np.asarray(got[f"out_{name}"]) for name, _ in _OUT}
    rnn = out["rnn_hold"].reshape(P, NJ, 8)
    ffn = out["ffn_hold"].reshape(P, 2 * NF, 4)

    def rows(v):
        return v.transpose(2, 1, 0).reshape(1, 1, v.shape[2], -1)

    return (out["y_prompt"].reshape(1, TP, D), out["y_sample"].reshape(1, TS, D),
            out["k_prompt"].transpose(2, 0, 1).reshape(1, 1, PAST, 8, HD),
            out["v_prompt"].reshape(1, 1, PAST, 8, HD),
            out["k_sample"].transpose(2, 0, 1).reshape(1, 1, TS, 8, HD),
            out["v_sample"].reshape(1, 1, TS, 8, HD),
            rows(rnn[:, :, 0:3]), rows(rnn[:, :, 3:6]),
            rows(rnn[:, :, 6:7]).reshape(1, 1, -1), rows(rnn[:, :, 7:8]).reshape(1, 1, -1),
            rows(ffn[:, :, 0:2]), rows(ffn[:, :, 2:4]))
```
